# Optimizing a Trainium2 kernel written in Bass

```python
import jax, jax.numpy as jnp
from jax import lax
import numpy as np

D_MODEL = 1024
BATCH = 1
SEQ = 128
DEPTH = 2
DEC_BATCH = 1
DEC_SEQ = 128
PAST_LEN = 128

GRID_W = 64
N_MIXERS = 2
N_CONV_LAYERS = (DEPTH + 1) // 2
N_ATTN_LAYERS = DEPTH // 2
CONV_WIDTH = 31
CONV_PAD = CONV_WIDTH // 2
N_HEADS = 16
N_KV_HEADS = 4
HEAD_DIM = 64
GQA_GROUP = N_HEADS // N_KV_HEADS
ATTN_WIDTH = N_HEADS * HEAD_DIM
WINDOW = 128
BAND_BLOCK = WINDOW
ROPE_THETA = 10000.0
ROPE_PAIRS = HEAD_DIM // 4
N_EXPERTS = 64
N_EXPERT_GROUPS = 8
TOPK_GROUPS = 4
TOP_K = 8
D_EXPERT = 256
D_SHARED = 256
ROUTED_SCALE = 2.5
MOE_BLOCK = 128
NORM_EPS = 1e-6
N_ADA = 6

kernel_name = 'hybrid_conv_swa_moe_diffusion_step'

def rms_norm(x, g):
    xf = x.astype(jnp.float32)
    y = xf * lax.rsqrt(jnp.mean(xf * xf, axis=-1, keepdims=True) + NORM_EPS)
    return (y * g.astype(jnp.float32)).astype(x.dtype)

def ada_params(cvec, w, b):
    m = jax.nn.silu(cvec) @ w + b
    return jnp.split(m, N_ADA, axis=-1)

def modulate(x, g, shift, scale):
    return rms_norm(x, g) * (1.0 + scale[:, None, :]) + shift[:, None, :]

def swiglu(x, wg, wu, wd):
    return (jax.nn.silu(x @ wg) * (x @ wu)) @ wd

def conv_module(h, w1, b1, wdw, bdw, gn, w2, b2):
    u = h @ w1 + b1
    a, gt = jnp.split(u, 2, axis=-1)
    u = a * jax.nn.sigmoid(gt)
    dw = lax.conv_general_dilated(u, wdw[:, None, :], window_strides=(1,),
                                  padding=[(CONV_PAD, CONV_PAD)],
                                  dimension_numbers=('NWC', 'WIO', 'NWC'),
                                  feature_group_count=u.shape[-1]) + bdw
    return jax.nn.silu(rms_norm(dw, gn)) @ w2 + b2

def rope2d(x):
    L = x.shape[1]
    rows = L // GRID_W
    row = jnp.repeat(jnp.arange(rows, dtype=jnp.float32), GRID_W)
    col = jnp.tile(jnp.arange(GRID_W, dtype=jnp.float32), rows)
    inv_freq = ROPE_THETA ** (-jnp.arange(ROPE_PAIRS, dtype=jnp.float32) / ROPE_PAIRS)

    def rot(y, pos):
        ang = pos[:, None] * inv_freq[None, :]
        cos = jnp.cos(ang)[None, :, None, :]
        sin = jnp.sin(ang)[None, :, None, :]
        yf = y.astype(jnp.float32)
        y1, y2 = yf[..., :ROPE_PAIRS], yf[..., ROPE_PAIRS:]
        return jnp.concatenate([y1 * cos - y2 * sin, y1 * sin + y2 * cos], axis=-1)

    half = HEAD_DIM // 2
    out = jnp.concatenate([rot(x[..., :half], row), rot(x[..., half:], col)], axis=-1)
    return out.astype(x.dtype)

def qkv_heads(h, wqkv, qn, kn):
    B, L, _ = h.shape
    qkv = h @ wqkv
    q = qkv[..., :ATTN_WIDTH].reshape(B, L, N_HEADS, HEAD_DIM)
    k = qkv[..., ATTN_WIDTH:ATTN_WIDTH + N_KV_HEADS * HEAD_DIM].reshape(B, L, N_KV_HEADS, HEAD_DIM)
    v = qkv[..., ATTN_WIDTH + N_KV_HEADS * HEAD_DIM:].reshape(B, L, N_KV_HEADS, HEAD_DIM)
    return rms_norm(q, qn), rms_norm(k, kn), v

def attn_context(h, wqkv, qn, kn, sink, wo):
    B, L, _ = h.shape
    q, k, v = qkv_heads(h, wqkv, qn, kn)
    qg = q.reshape(B, L, N_KV_HEADS, GQA_GROUP, HEAD_DIM)
    s = jnp.einsum('bqkgd,bskd->bkgqs', qg, k, preferred_element_type=jnp.float32) * (HEAD_DIM ** -0.5)
    s_sink = jnp.broadcast_to(sink.astype(jnp.float32).reshape(N_KV_HEADS, GQA_GROUP)[None, :, :, None, None],
                              s.shape[:-1] + (1,))
    p = jax.nn.softmax(jnp.concatenate([s, s_sink], axis=-1), axis=-1)[..., :L]
    o = jnp.einsum('bkgqs,bskd->bqkgd', p.astype(v.dtype), v).reshape(B, L, ATTN_WIDTH)
    return o @ wo, k, v

def band_mask(nb, L):
    a = jnp.arange(BAND_BLOCK)[:, None]
    b = jnp.arange(3 * BAND_BLOCK)[None, :]
    rel = b - BAND_BLOCK - a
    kpos = (jnp.arange(nb)[:, None, None] - 1) * BAND_BLOCK + b[None]
    return (jnp.abs(rel) <= WINDOW)[None] & (kpos >= 0) & (kpos < L)

def attn_latent(h, k_ctx, v_ctx, wqkv, qn, kn, sink, wo):
    B, L, _ = h.shape
    q, k, v = qkv_heads(h, wqkv, qn, kn)
    q, k = rope2d(q), rope2d(k)
    nb = L // BAND_BLOCK
    pad = ((0, 0), (BAND_BLOCK, BAND_BLOCK), (0, 0), (0, 0))
    kb = jnp.pad(k, pad).reshape(B, nb + 2, BAND_BLOCK, N_KV_HEADS, HEAD_DIM)
    vb = jnp.pad(v, pad).reshape(B, nb + 2, BAND_BLOCK, N_KV_HEADS, HEAD_DIM)
    k_band = jnp.concatenate([kb[:, :-2], kb[:, 1:-1], kb[:, 2:]], axis=2)
    v_band = jnp.concatenate([vb[:, :-2], vb[:, 1:-1], vb[:, 2:]], axis=2)
    qb = q.reshape(B, nb, BAND_BLOCK, N_KV_HEADS, GQA_GROUP, HEAD_DIM)
    scale = HEAD_DIM ** -0.5
    s_loc = jnp.einsum('bnqkgd,bnskd->bnkgqs', qb, k_band, preferred_element_type=jnp.float32) * scale
    mask = band_mask(nb, L)[None, :, None, None]
    s_loc = jnp.where(mask, s_loc, -jnp.inf)
    s_ctx = jnp.einsum('bnqkgd,bckd->bnkgqc', qb, k_ctx, preferred_element_type=jnp.float32) * scale
    s_sink = jnp.broadcast_to(sink.astype(jnp.float32).reshape(N_KV_HEADS, GQA_GROUP)[None, None, :, :, None, None],
                              s_loc.shape[:-1] + (1,))
    p = jax.nn.softmax(jnp.concatenate([s_loc, s_ctx, s_sink], axis=-1), axis=-1)
    nl = 3 * BAND_BLOCK
    lc = k_ctx.shape[1]
    p_loc = p[..., :nl].astype(v.dtype)
    p_ctx = p[..., nl:nl + lc].astype(v.dtype)
    o = (jnp.einsum('bnkgqs,bnskd->bnqkgd', p_loc, v_band)
         + jnp.einsum('bnkgqc,bckd->bnqkgd', p_ctx, v_ctx.astype(v.dtype)))
    return o.reshape(B, L, ATTN_WIDTH) @ wo

def routed_experts(x, eidx, wsel, wg, wu, wd):
    T, D = x.shape
    tk = T * TOP_K
    n_blocks = -(-tk // MOE_BLOCK) + N_EXPERTS
    e_flat = eidx.reshape(-1)
    tok_flat = jnp.repeat(jnp.arange(T, dtype=jnp.int32), TOP_K)
    w_flat = wsel.reshape(-1)
    order = jnp.argsort(e_flat)
    e_sorted = e_flat[order]
    counts = jnp.bincount(e_flat, length=N_EXPERTS)
    padded = (counts + MOE_BLOCK - 1) // MOE_BLOCK * MOE_BLOCK
    start = jnp.cumsum(counts) - counts
    pad_end = jnp.cumsum(padded)
    pad_start = pad_end - padded
    dest = pad_start[e_sorted] + jnp.arange(tk) - start[e_sorted]
    slot_tok = jnp.full((n_blocks * MOE_BLOCK,), T, jnp.int32).at[dest].set(tok_flat[order])
    slot_w = jnp.zeros((n_blocks * MOE_BLOCK,), jnp.float32).at[dest].set(w_flat[order])
    block_exp = jnp.minimum(jnp.searchsorted(pad_end, jnp.arange(n_blocks) * MOE_BLOCK, side='right'),
                            N_EXPERTS - 1)
    x_pad = jnp.concatenate([x, jnp.zeros((1, D), x.dtype)], axis=0)
    xs = x_pad[slot_tok].reshape(n_blocks, MOE_BLOCK, D)

    def expert_block(args):
        xb, e = args
        return swiglu(xb, wg[e], wu[e], wd[e])

    ys = lax.map(expert_block, (xs, block_exp)).reshape(-1, D)
    out = jnp.zeros((T + 1, D), x.dtype).at[slot_tok].add(ys * slot_w[:, None].astype(x.dtype))
    return out[:T]

def moe(h, router_w, router_bias, wg, wu, wd, sg, su, sd):
    B, L, D = h.shape
    x = h.reshape(B * L, D)
    T = B * L
    scores = jax.nn.sigmoid(jnp.einsum('td,de->te', x, router_w, preferred_element_type=jnp.float32))
    choice = scores + router_bias.astype(jnp.float32)
    grp = choice.reshape(T, N_EXPERT_GROUPS, N_EXPERTS // N_EXPERT_GROUPS)
    gscore = lax.top_k(grp, 2)[0].sum(-1)
    _, gidx = lax.top_k(gscore, TOPK_GROUPS)
    gmask = jax.nn.one_hot(gidx, N_EXPERT_GROUPS, dtype=jnp.float32).sum(1) > 0
    emask = jnp.repeat(gmask, N_EXPERTS // N_EXPERT_GROUPS, axis=1)
    _, eidx = lax.top_k(jnp.where(emask, choice, -jnp.inf), TOP_K)
    wsel = jnp.take_along_axis(scores, eidx, axis=1)
    wsel = wsel / jnp.sum(wsel, axis=-1, keepdims=True) * ROUTED_SCALE
    routed = routed_experts(x, eidx, wsel, wg, wu, wd)
    return (routed + swiglu(x, sg, su, sd)).reshape(B, L, D)

def setup_inputs(seed: int = 0) -> dict:
    key = jax.random.key(seed)
    ks = jax.random.split(key, 32)
    f32 = jnp.float32
    D = D_MODEL
    nrm = lambda k, shape, s: jax.random.normal(k, shape, f32) * s
    return {
        'x_prompt': nrm(ks[0], (BATCH, SEQ, D), 1.0),
        'x_sample': nrm(ks[1], (DEC_BATCH, DEC_SEQ, D), 1.0),
        'cache_k': nrm(ks[2], (DEC_BATCH, N_ATTN_LAYERS, PAST_LEN, N_KV_HEADS, HEAD_DIM), 1.0),
        'cache_v': nrm(ks[3], (DEC_BATCH, N_ATTN_LAYERS, PAST_LEN, N_KV_HEADS, HEAD_DIM), 1.0),
        'c': nrm(ks[4], (DEC_BATCH, D), 1.0),
        'c_ctx': nrm(ks[5], (D,), 1.0),
        'ada_w': nrm(ks[6], (DEPTH, D, N_ADA * D), 0.5 * D ** -0.5),
        'ada_b': nrm(ks[7], (DEPTH, N_ADA * D), 0.02),
        'norm_mix': 1.0 + nrm(ks[8], (DEPTH, D), 0.01),
        'norm_ffn': 1.0 + nrm(ks[9], (DEPTH, D), 0.01),
        'conv_w1': nrm(ks[10], (N_CONV_LAYERS, D, 2 * D), D ** -0.5),
        'conv_b1': nrm(ks[11], (N_CONV_LAYERS, 2 * D), 0.02),
        'conv_dw': nrm(ks[12], (N_CONV_LAYERS, CONV_WIDTH, D), CONV_WIDTH ** -0.5),
        'conv_dw_b': nrm(ks[13], (N_CONV_LAYERS, D), 0.02),
        'conv_norm': 1.0 + nrm(ks[14], (N_CONV_LAYERS, D), 0.01),
        'conv_w2': nrm(ks[15], (N_CONV_LAYERS, D, D), D ** -0.5),
        'conv_b2': nrm(ks[16], (N_CONV_LAYERS, D), 0.02),
        'attn_wqkv': nrm(ks[17], (N_ATTN_LAYERS, D, ATTN_WIDTH + 2 * N_KV_HEADS * HEAD_DIM), D ** -0.5),
        'attn_q_norm': 1.0 + nrm(ks[18], (N_ATTN_LAYERS, HEAD_DIM), 0.01),
        'attn_k_norm': 1.0 + nrm(ks[19], (N_ATTN_LAYERS, HEAD_DIM), 0.01),
        'attn_sink': nrm(ks[20], (N_ATTN_LAYERS, N_HEADS), 0.5),
        'attn_wo': nrm(ks[21], (N_ATTN_LAYERS, ATTN_WIDTH, D), ATTN_WIDTH ** -0.5),
        'router_w': nrm(ks[22], (DEPTH, D, N_EXPERTS), D ** -0.5),
        'router_bias': nrm(ks[23], (DEPTH, N_EXPERTS), 0.01),
        'exp_w_gate': nrm(ks[24], (DEPTH, N_EXPERTS, D, D_EXPERT), D ** -0.5),
        'exp_w_up': nrm(ks[25], (DEPTH, N_EXPERTS, D, D_EXPERT), D ** -0.5),
        'exp_w_down': nrm(ks[26], (DEPTH, N_EXPERTS, D_EXPERT, D), D_EXPERT ** -0.5),
        'sh_w_gate': nrm(ks[27], (DEPTH, D, D_SHARED), D ** -0.5),
        'sh_w_up': nrm(ks[28], (DEPTH, D, D_SHARED), D ** -0.5),
        'sh_w_down': nrm(ks[29], (DEPTH, D_SHARED, D), D_SHARED ** -0.5),
    }

def reference(x_prompt, x_sample, cache_k, cache_v, c, c_ctx,
              ada_w, ada_b, norm_mix, norm_ffn,
              conv_w1, conv_b1, conv_dw, conv_dw_b, conv_norm, conv_w2, conv_b2,
              attn_wqkv, attn_q_norm, attn_k_norm, attn_sink, attn_wo,
              router_w, router_bias, exp_w_gate, exp_w_up, exp_w_down,
              sh_w_gate, sh_w_up, sh_w_down):
    y_p = x_prompt
    y_s = x_sample
    k_list = []
    v_list = []
    for i in range(DEPTH):
        sh1_p, sc1_p, g1_p, sh2_p, sc2_p, g2_p = ada_params(c_ctx[None, :], ada_w[i], ada_b[i])
        sh1_s, sc1_s, g1_s, sh2_s, sc2_s, g2_s = ada_params(c, ada_w[i], ada_b[i])
        hp = modulate(y_p, norm_mix[i], sh1_p, sc1_p)
        hs = modulate(y_s, norm_mix[i], sh1_s, sc1_s)
        j = i // N_MIXERS
        if i % N_MIXERS == 0:
            cp = (conv_w1[j], conv_b1[j], conv_dw[j], conv_dw_b[j], conv_norm[j], conv_w2[j], conv_b2[j])
            mp = conv_module(hp, *cp)
            ms = conv_module(hs, *cp)
        else:
            ap = (attn_wqkv[j], attn_q_norm[j], attn_k_norm[j], attn_sink[j], attn_wo[j])
            mp, kc, vc = attn_context(hp, *ap)
            k_list.append(kc)
            v_list.append(vc)
            ms = attn_latent(hs, cache_k[:, j], cache_v[:, j], *ap)
        y_p = y_p + g1_p[:, None, :] * mp
        y_s = y_s + g1_s[:, None, :] * ms
        mw = (router_w[i], router_bias[i], exp_w_gate[i], exp_w_up[i], exp_w_down[i],
              sh_w_gate[i], sh_w_up[i], sh_w_down[i])
        y_p = y_p + g2_p[:, None, :] * moe(modulate(y_p, norm_ffn[i], sh2_p, sc2_p), *mw)
        y_s = y_s + g2_s[:, None, :] * moe(modulate(y_s, norm_ffn[i], sh2_s, sc2_s), *mw)
    new_k = jnp.stack(k_list, axis=1)
    new_v = jnp.stack(v_list, axis=1)
    return (y_p, y_s, new_k, new_v)


_drawn_inputs = setup_inputs


def setup_inputs(seed=0):
    import zlib

    import numpy as np

    out = dict(_drawn_inputs(seed))
    spreads = {}
    factors = {'norm_mix': 3.822, 'attn_q_norm': 6.73, 'attn_k_norm': 5.151, 'attn_sink': 6.447}
    for name, (base, spread) in spreads.items():
        noise = np.random.default_rng([zlib.crc32(name.encode()), seed]).standard_normal(out[name].shape)
        drawn = base * np.exp(spread * noise) if base else spread * noise
        out[name] = __import__('jax').numpy.asarray(drawn.astype(out[name].dtype))
    for name, factor in factors.items():
        out[name] = (out[name] * factor).astype(out[name].dtype)
    return out
```

```python
from contextlib import ExitStack

import concourse.bass as bass
from concourse import mybir

F32 = mybir.dt.float32
BF16 = mybir.dt.bfloat16
I32 = mybir.dt.int32
ALU = mybir.AluOpType
ACT = mybir.ActivationFunctionType
AX_X = mybir.AxisListType.X

P = 128
D = 1024
KC = D // P
T = 128
G = 2
TT = G * T
L = 2
NADA = 6
TAPS = 31
PAD = TAPS // 2
NH, NKV, HD = 16, 4, 64
QG = NH // NKV
QKVW = (NH + 2 * NKV) * HD
NE, NGRP, TOPG, TOPK = 64, 8, 4, 8
EPG = NE // NGRP
DE = 256
FC = DE // P
ROUTED_SCALE = 2.5
EPS = 1e-6
SLOTS = 64
PAIRS = NE // 2
MAXOVF = TT * TOPK // (SLOTS + 1) + 1
OVF_PAIRS = MAXOVF // 2
BIG = 1e30
EW = 3 * D * DE // P

C_ID, C_ONE, C_U, C_IOTA, C_TRI, C_COS, C_SIN = 0, 128, 256, 384, 448, 512, 576
C_W = 640


def build_kernel(nc, x_prompt, x_sample, cache_k, cache_v, c, c_ctx, ada_w, ada_b, norm_mix, norm_ffn,
                 conv_w1, conv_b1, conv_dw, conv_dw_b, conv_norm, conv_w2, conv_b2,
                 attn_wqkv, attn_q_norm, attn_k_norm, attn_sink, attn_wo,
                 router_w, router_bias, exp_w_gate, exp_w_up, exp_w_down,
                 sh_w_gate, sh_w_up, sh_w_down, consts, y_prompt, y_sample, new_k, new_v):
    with ExitStack() as ctx:
        def sb(name, shape, dt=F32):
            return ctx.enter_context(nc.sbuf_tensor(name, shape, dt))

        def sem(name):
            return ctx.enter_context(nc.semaphore(name))

        cst = sb("cst", [P, C_W])
        ident = cst[:, C_ID:C_ID + P]
        ones = cst[:, C_ONE:C_ONE + P]
        iota = cst[:, C_IOTA:C_IOTA + SLOTS]
        tri = cst[:, C_TRI:C_TRI + 64]
        cosT = cst[:, C_COS:C_COS + 32]
        sinT = cst[:, C_SIN:C_SIN + 32]
        ubf = sb("ubf", [P, 2, P], BF16)
        yT = sb("yT", [P, KC, TT])
        hT = sb("hT", [P, KC, TT])
        hbf = sb("hbf", [P, 3, G, KC, P], BF16)
        rstd = sb("rstd", [P, TT])
        epsc = sb("epsc", [P, 1])
        cT = sb("cT", [P, 2, KC])
        scT = sb("scT", [P, KC, 32])
        mod = sb("mod", [P, L, 2, NADA * KC])
        modA = sb("modA", [P, L, 2, 2, KC])
        adab = sb("adab", [P, L, NADA, KC])
        gains = sb("gains", [P, L, 2, KC])
        b1c = sb("b1c", [P, 2, KC])
        dwc = sb("dwc", [P, TAPS, KC])
        cvec = sb("cvec", [P, 3, KC])
        qkn = sb("qkn", [P, 2, HD])
        sinkb = sb("sinkb", [P, NH])
        rbias = sb("rbias", [P, L, NE])
        rw = sb("rw", [P, L, KC, NE])
        scores = sb("scores", [P, G, NE])
        gsc = sb("gsc", [P, G, NGRP])
        sel = sb("sel", [P, G, NE])
        selb = sb("selb", [P, G, NE], BF16)
        wt = sb("wt", [P, G, NE])
        wsum = sb("wsum", [P, G, 2])
        rank = sb("rank", [P, G, NE])
        ovrank = sb("ovrank", [P, G, NE])
        novc = sb("novc", [NE, 8])
        novb = sb("novb", [NE, P], BF16)
        ovl = sb("ovl", [NE, MAXOVF], BF16)
        endc = sb("endc", [NE, 1])
        table = sb("table", [1, 1 + MAXOVF], I32)
        ring = sb("ring", [P, 4, EW])
        S = sb("S", [P, 12288])
        W = sb("W", [P, 4608])

        ring_f = ring[:, :, :].rearrange("p s n -> p (s n)")
        w1 = ring_f[:, 0:16384].rearrange("p (k n) -> p k n", k=KC)
        w2 = ring_f[:, 16384:24576].rearrange("p (k n) -> p k n", k=KC)
        ada = S[:, :].rearrange("p (s n) -> p s n", s=2)
        wqkv = S[:, :].rearrange("p (k n) -> p k n", k=KC)
        wo = S[:, 0:8192].rearrange("p (k n) -> p k n", k=KC)
        shw = S[:, 0:EW]

        def gate_of(w):
            return w[:, 0:2048].rearrange("p (k f) -> p k f", k=KC)

        def up_of(w):
            return w[:, 2048:4096].rearrange("p (k f) -> p k f", k=KC)

        def down_of(w):
            return w[:, 4096:6144].rearrange("p (j n) -> p j n", j=FC)

        xg = W[:, 0:1024].rearrange("p (k s) -> p k s", k=KC)
        shh = W[:, 0:1024].rearrange("p (j t) -> p j t", j=4)
        gbf = W[:, 1024:1152].bitcast(BF16).rearrange("p (g s) -> p g s", g=G)
        gw = W[:, 1152:1408].rearrange("p (g s) -> p g s", g=G)
        comb = W[:, 1408:1920].rearrange("p (b t) -> p b t", b=2)
        silu_h = W[:, 1920:2176]
        hid = W[:, 2176:2432]
        hidT = W[:, 2432:2688].rearrange("p (j s) -> p j s", j=FC)
        ysb = W[:, 2688:3712].rearrange("p (k m) -> p k m", k=KC)
        zer = W[:, 3712:3840]
        choice = W[:, 1408:1536].rearrange("p (g e) -> p g e", g=G)
        top8 = W[:, 1536:1664].rearrange("p (g r n) -> p g r n", g=G, r=NGRP)
        gcmp = W[:, 1664:1792].rearrange("p (g r n) -> p g r n", g=G, r=NGRP)
        gcmp2 = W[:, 1792:1920].rearrange("p (g r n) -> p g r n", g=G, r=NGRP)
        upad = W[:, 0:KC * G * (T + 2 * PAD)].rearrange("p (c g t) -> p c g t", c=KC, g=G)
        dwo = W[:, 2560:4608].rearrange("p (c t) -> p c t", c=KC)
        hb_f = hbf[:, :, :, :, :].rearrange("p s g k m -> p (s g k m)").bitcast(F32)
        sq = hb_f[:, 0:2048].rearrange("p (k t) -> p k t", k=KC)
        sgt = hb_f[:, 2048:2560].rearrange("p (b t) -> p b t", b=2)
        tmp2 = sgt
        arow = hT[:, 0:6, :].rearrange("p k t -> p (k t)").rearrange("p (b n) -> p b n", b=3)
        xtok = ring_f[:, 16384 - 2048:16384].rearrange("p (g n) -> p g n", g=G)
        ytok = ring_f[:, 0:2048].rearrange("p (g n) -> p g n", g=G)
        B0 = 2 * EW
        qkv = ring_f[:, B0:B0 + 3072].rearrange("p (g n) -> p g n", g=G)
        asq = ring_f[:, B0 + 3072:B0 + 5632].rearrange("p (g n) -> p g n", g=G)
        prob = ring_f[:, B0 + 3072:B0 + 5120].rearrange("p (b h s) -> p b h s", b=2, h=QG)
        otok = ring_f[:, B0 + 6912:B0 + 8960].rearrange("p (g n) -> p g n", g=G)
        oT = ring_f[:, B0 + 8960:B0 + 11008].rearrange("p (k t) -> p k t", k=KC)
        vctx = ring_f[:, B0 + 11008:B0 + 11264]
        kctx = ring_f[:, B0 + 11264:B0 + 11520]
        stat = ring_f[:, B0 + 11520:B0 + 11776]
        qTt = W[:, 0:2048].rearrange("p (c t) -> p c t", c=KC)
        kTt = W[:, 2048:2816].rearrange("p (c t) -> p c t", c=2)
        probT = hb_f[:, 0:1024].rearrange("p (b n) -> p b n", b=2)

        ps = [ctx.enter_context(nc.psum_tensor(f"ps{i}", [P, 512], F32)) for i in range(8)]
        PG, PT, PGU, PY = ps[0], ps[1], ps[2], ps[3]
        acc = ps[4:8]

        dve_step, act_step = sem("dve_step"), sem("act_step")
        ld_const, ld_x, ld_small, ld_cond = sem("ld_const"), sem("ld_x"), sem("ld_small"), sem("ld_cond")
        ld_ada = [sem(f"ld_ada{i}") for i in range(2)]
        ld_w1, ld_w2, ld_qkv, ld_kv, ld_wo = sem("ld_w1"), sem("ld_w2"), sem("ld_qkv"), sem("ld_kv"), sem("ld_wo")
        ld_sh = sem("ld_sh")
        stored = sem("stored")
        cond_ready, cond_zero = sem("cond_ready"), sem("cond_zero")
        ada_used, ada_rows, ada_cols, mod_ready = sem("ada_used"), sem("ada_rows"), sem("ada_cols"), sem("mod_ready")
        x_tr, x_in = sem("x_tr"), sem("x_in")
        bf_const = sem("bf_const")
        sq_ready, ss_ready, root_ready, h_ready = sem("sq_ready"), sem("ss_ready"), sem("root_ready"), sem("h_ready")
        cv_u, cv_gate, cv_in, cv_out = sem("cv_u"), sem("cv_gate"), sem("cv_in"), sem("cv_out")
        cn_scaled, cn_ready = sem("cn_scaled"), sem("cn_ready")
        pj_out, pj_bias, pj_done = sem("pj_out"), sem("pj_bias"), sem("pj_done")
        at_qkv, at_copied, at_qk, at_root, at_nrm, at_tr, at_trc = (
            sem("at_qkv"), sem("at_copied"), sem("at_qk"), sem("at_root"), sem("at_nrm"), sem("at_tr"), sem("at_trc"))
        at_s, at_max, at_exp, at_pt, at_ptc, at_o, at_on, at_ot, at_otc = (
            sem("at_s"), sem("at_max"), sem("at_exp"), sem("at_pt"), sem("at_ptc"), sem("at_o"), sem("at_on"),
            sem("at_ot"), sem("at_otc"))
        rt_logits, rt_score, rt_sel, rt_rank, rt_nov, rt_pos, rt_list, rt_tab, rt_table = (
            sem("rt_logits"), sem("rt_score"), sem("rt_sel"), sem("rt_rank"), sem("rt_nov"), sem("rt_pos"),
            sem("rt_list"), sem("rt_tab"), sem("rt_table"))
        ht_tr, ht_b1, ht_r1, ht_b2, ht_done = (
            sem("ht_tr"), sem("ht_b1"), sem("ht_r1"), sem("ht_b2"), sem("ht_done"))
        sh_gu, sh_silu, sh_hid, sh_done = sem("sh_gu"), sem("sh_silu"), sem("sh_hid"), sem("sh_done")
        zeroed = sem("zeroed")
        moe_done, y_ready = sem("moe_done"), sem("y_ready")
        y_tr, y_out = sem("y_tr"), sem("y_out")
        ld_gu = [[sem(f"ld_gu{l}_{s}") for s in range(4)] for l in range(L)]
        ld_dn = [[sem(f"ld_dn{l}_{s}") for s in range(4)] for l in range(L)]
        pe_gather = [sem(f"pe_gather{l}") for l in range(L)]
        pe_gu = [sem(f"pe_gu{l}") for l in range(L)]
        pe_ct = [sem(f"pe_ct{l}") for l in range(L)]
        pe_ht = [sem(f"pe_ht{l}") for l in range(L)]
        pe_dn = [sem(f"pe_dn{l}") for l in range(L)]
        pe_comb = [sem(f"pe_comb{l}") for l in range(L)]
        act_xg = [sem(f"act_xg{l}") for l in range(L)]
        act_silu = [sem(f"act_silu{l}") for l in range(L)]
        act_y = [sem(f"act_y{l}") for l in range(L)]
        dve_g = [sem(f"dve_g{l}") for l in range(L)]
        dve_gw = [sem(f"dve_gw{l}") for l in range(L)]
        dve_c = [sem(f"dve_c{l}") for l in range(L)]
        dve_h = [sem(f"dve_h{l}") for l in range(L)]
        dve_ht = [sem(f"dve_ht{l}") for l in range(L)]
        dve_y = [sem(f"dve_y{l}") for l in range(L)]
        dve_ov = [sem(f"dve_ov{l}") for l in range(L)]

        block = ctx.enter_context(nc.Block())

        @block.sync
        def _(sp):
            def cols(v):
                return v.rearrange("(p k) -> p k", k=KC)

            sp.dma_start(cT[:, 0, :], cols(c_ctx)).then_inc(ld_cond, 16)
            sp.dma_start(cT[:, 1, :], cols(c[0])).then_inc(ld_cond, 16)
            sp.dma_start(cst[:, :], consts).then_inc(ld_const, 16)

            def load_ada(l):
                rows = ada_w[l].rearrange("(p k) n -> k p n", k=KC)
                for k in range(KC):
                    n = l * KC + k
                    if n >= 2:
                        sp.wait_ge(ada_used, n - 1)
                    sp.dma_start(ada[:, n % 2, :], rows[k]).then_inc(ld_ada[n % 2], 16)

            def load_expert(l, e, s, part):
                w = ring[:, s, :]
                if part == "gu":
                    sp.dma_start(w[:, 0:2048], exp_w_gate[l, e].rearrange("(p k) f -> p (k f)", k=KC)
                                 ).then_inc(ld_gu[l][s], 16)
                    sp.dma_start(w[:, 2048:4096], exp_w_up[l, e].rearrange("(p k) f -> p (k f)", k=KC)
                                 ).then_inc(ld_gu[l][s], 16)
                else:
                    sp.dma_start(w[:, 4096:6144], exp_w_down[l, e].rearrange("(p j) n -> p (j n)", j=FC)
                                 ).then_inc(ld_dn[l][s], 16)

            def load_expert_at(l, e, s, part):
                w = ring[:, s, :]
                if part == "gu":
                    for o, src in ((0, exp_w_gate), (2048, exp_w_up)):
                        sp.dma_start(w[:, o:o + 2048],
                                     src[l, bass.ds(e, 1)].rearrange("e (p k) f -> (e p) (k f)", k=KC)
                                     ).then_inc(ld_gu[l][s], 16)
                else:
                    sp.dma_start(w[:, 4096:6144],
                                 exp_w_down[l, bass.ds(e, 1)].rearrange("e (p j) n -> (e p) (j n)", j=FC)
                                 ).then_inc(ld_dn[l][s], 16)

            def load_shared(l):
                sp.dma_start(shw[:, 0:2048], sh_w_gate[l].rearrange("(p k) f -> p (k f)", k=KC)).then_inc(ld_sh, 16)
                sp.dma_start(shw[:, 2048:4096], sh_w_up[l].rearrange("(p k) f -> p (k f)", k=KC)).then_inc(ld_sh, 16)
                sp.dma_start(shw[:, 4096:6144], sh_w_down[l].rearrange("(p j) n -> p (j n)", j=FC)
                             ).then_inc(ld_sh, 16)

            sp.dma_start(xtok[:, 0, :], x_prompt[0]).then_inc(ld_x, 16)
            sp.dma_start(xtok[:, 1, :], x_sample[0]).then_inc(ld_x, 16)
            load_ada(0)
            sp.wait_ge(x_tr, 4)
            sp.dma_start(w1, conv_w1[0].rearrange("(p k) n -> p k n", k=KC)).then_inc(ld_w1, 16)
            sp.dma_start(w2, conv_w2[0].rearrange("(p k) n -> p k n", k=KC)).then_inc(ld_w2, 16)
            load_ada(1)
            sp.wait_ge(ada_used, 2 * KC)
            load_shared(0)

            for l in range(L):
                if l == 0:
                    sp.wait_ge(cv_u, KC)
                else:
                    sp.wait_ge(sh_done, 1)
                    sp.dma_start(wqkv, attn_wqkv[0].rearrange("(p k) n -> p k n", k=KC)).then_inc(ld_qkv, 16)
                    sp.wait_ge(moe_done, 1)
                    sp.dma_start(kctx, cache_k[0, 0].rearrange("t h d -> t (h d)")).then_inc(ld_kv, 16)
                    sp.dma_start(vctx, cache_v[0, 0].rearrange("t h d -> t (h d)")).then_inc(ld_kv, 16)
                for s in range(2):
                    load_expert(l, s, s, "gu")
                for s in range(2):
                    load_expert(l, s, s, "dn")
                if l == 0:
                    sp.wait_ge(pj_out, 4)
                else:
                    sp.wait_ge(at_nrm, 2)
                    sp.wait_ge(at_copied, 2)
                    sp.dma_start(new_k[0, 0].rearrange("t h d -> t (h d)"),
                                 qkv[:, 0, NH * HD:(NH + NKV) * HD]).then_inc(stored, 16)
                    sp.dma_start(new_v[0, 0].rearrange("t h d -> t (h d)"),
                                 qkv[:, 0, (NH + NKV) * HD:QKVW]).then_inc(stored, 16)
                    sp.wait_ge(at_qkv, 6)
                    sp.dma_start(wo, attn_wo[0].rearrange("(p k) n -> p k n", k=KC)).then_inc(ld_wo, 16)
                    sp.wait_ge(pj_out, 8)
                    load_shared(1)
                    sp.wait_ge(stored, 32)
                for s in range(2, 4):
                    load_expert(l, s, s, "gu")
                for s in range(2, 4):
                    load_expert(l, s, s, "dn")
                with sp.Fori(1, PAIRS // 2) as it:
                    for half in range(2):
                        sp.wait_ge(pe_gu[l], 2 * it + half - 1)
                        for b in range(2):
                            load_expert_at(l, 4 * it + 2 * half + b, 2 * half + b, "gu")
                        sp.wait_ge(pe_dn[l], 4 * it + 2 * half - 2)
                        for b in range(2):
                            load_expert_at(l, 4 * it + 2 * half + b, 2 * half + b, "dn")
                sp.wait_ge(rt_table, l + 1)
                nov = sp.value_load(table[0:1, 0:1], min_val=0, max_val=MAXOVF)
                with sp.Fori(0, OVF_PAIRS // 2) as it:
                    for half in range(2):
                        with sp.If(nov > 4 * it + 2 * half):
                            e = [sp.value_load(table[0:1, bass.ds(4 * it + 2 * half + b + 1, 1)],
                                               min_val=0, max_val=NE - 1) for b in range(2)]
                            sp.wait_ge(pe_gu[l], 2 * it + half + PAIRS - 1)
                            for b in range(2):
                                load_expert_at(l, e[b], 2 * half + b, "gu")
                            sp.wait_ge(pe_dn[l], 4 * it + 2 * half + 2 * PAIRS - 2)
                            for b in range(2):
                                load_expert_at(l, e[b], 2 * half + b, "dn")
            for g, y in enumerate((y_prompt, y_sample)):
                sp.wait_ge(y_out, 2 * (g + 1))
                sp.dma_start(y[0], ytok[:, g, :]).then_inc(stored, 16)
            sp.wait_ge(stored, 64)

        @block.gpsimd
        def _(pool):
            def load(dst, src):
                pool.dma_start(dst, src).then_inc(ld_small, 16)

            for l in range(L):
                load(adab[:, l], ada_b[l].rearrange("(s p k) -> p s k", s=NADA, k=KC))
                load(gains[:, l, 0], norm_mix[l].rearrange("(p k) -> p k", k=KC))
                load(gains[:, l, 1], norm_ffn[l].rearrange("(p k) -> p k", k=KC))
                load(rbias[:, l], router_bias[l:l + 1, :].to_broadcast([P, NE]))
                load(rw[:, l], router_w[l].rearrange("(p k) e -> p k e", k=KC))
            load(b1c[:, :, :], conv_b1[0].rearrange("(h p k) -> p h k", h=2, k=KC))
            load(dwc[:, :, :], conv_dw[0].rearrange("j (p k) -> p j k", k=KC))
            for i, v in enumerate((conv_dw_b, conv_norm, conv_b2)):
                load(cvec[:, i], v[0].rearrange("(p k) -> p k", k=KC))
            load(qkn[:, 0], attn_q_norm[0:1, :].to_broadcast([P, HD]))
            load(qkn[:, 1], attn_k_norm[0:1, :].to_broadcast([P, HD]))
            load(sinkb[:, :], attn_sink[0:1, :].to_broadcast([P, NH]))

        N_SMALL = 5 * L + 2 + 3 + 3

        @block.tensor
        def _(pe):
            def ada_products(l):
                for k in range(KC):
                    n = l * KC + k
                    pe.wait_ge(ld_ada[n % 2], 16 * (n // 2 + 1))
                    for b in range(3):
                        for j in range(4):
                            rhs = ada[:, n % 2, (2 * b + j // 2) * D:(2 * b + j // 2 + 1) * D].rearrange(
                                "p (m q) -> p q m", q=KC)[:, 4 * (j % 2):4 * (j % 2) + 4, :]
                            mm = pe.matmul(ps[b][32 * j:32 * j + 32, :].rearrange("p (q m) -> p q m", q=4),
                                           scT[:, k, :], rhs, start=(k == 0), stop=(k == KC - 1))
                    mm.then_inc(ada_used, 1)

            def ada_transposes(l):
                for b in range(3):
                    pe.wait_ge(ada_rows, 3 * l + b + 1)
                    for q in range(4):
                        mm = pe.transpose(ps[b][:, q * P:(q + 1) * P], arow[:, b, q * P:(q + 1) * P], ident)
                    mm.then_inc(ada_cols, 1)

            def sum_squares(n, bank):
                pe.wait_ge(sq_ready, n)
                for k in range(KC):
                    mm = pe.matmul(ps[bank][:, 0:TT], ones, sq[:, k, :], start=(k == 0), stop=(k == KC - 1))
                mm.then_inc(ss_ready, 1)

            def project(w, x, ready, value, loaded):
                pe.wait_ge(loaded, 16)
                pe.wait_ge(ready, value)
                for b in range(4):
                    for h in range(2):
                        for k in range(KC):
                            mm = pe.matmul(ps[3 + b][:, h * TT:(h + 1) * TT],
                                           w[:, k, :].rearrange("p (m q) -> p q m", q=KC)[:, 2 * b + h, :],
                                           x[:, k, :], start=(k == 0), stop=(k == KC - 1))
                    mm.then_inc(pj_out, 1)

            pe.wait_ge(ld_const, 16)
            pe.wait_ge(ld_x, 32)
            for b in range(4):
                for h in range(2):
                    for g in range(G):
                        mm = pe.transpose(ps[3 + b][:, (2 * h + g) * T:(2 * h + g + 1) * T],
                                          xtok[:, g, :].rearrange("p (m q) -> p q m", q=KC)[:, 2 * b + h, :], ident)
                mm.then_inc(x_tr, 1)
            pe.wait_ge(cond_ready, 1)
            ada_products(0)
            ada_transposes(0)

            for l in range(L):
                sum_squares(1 if l == 0 else 4, 7)
                pe.wait_ge(h_ready, 2 * l + 1)
                if l == 0:
                    pe.wait_ge(ld_w1, 16)
                    pe.wait_ge(x_in, 4)
                    for cc in range(KC):
                        if cc >= 4:
                            pe.wait_ge(cv_in, cc - 3)
                        for h in range(2):
                            for k in range(KC):
                                mm = pe.matmul(ps[3 + cc % 4][:, h * TT:(h + 1) * TT],
                                               w1[:, k, h * D:(h + 1) * D].rearrange("p (m q) -> p q m", q=KC)[:, cc, :],
                                               hT[:, k, :], start=(k == 0), stop=(k == KC - 1))
                        mm.then_inc(cv_u, 1)
                    ada_products(1)
                    ada_transposes(1)
                    sum_squares(2, 7)
                    project(w2, dwo, cn_ready, KC, ld_w2)
                else:
                    pe.wait_ge(ld_qkv, 16)
                    for g in range(G):
                        for n in range(3):
                            i = 3 * g + n
                            for k in range(KC):
                                mm = pe.matmul(ps[i][:, :], hT[:, k, g * T:(g + 1) * T],
                                               wqkv[:, k, n * 512:(n + 1) * 512], start=(k == 0), stop=(k == KC - 1))
                            mm.then_inc(at_qkv, 1)
                    pe.wait_ge(ld_kv, 32)
                    for j in range(2):
                        mm = pe.transpose(ps[6][:, j * P:(j + 1) * P], kctx[:, j * P:(j + 1) * P], ident)
                    mm.then_inc(at_tr, 1)
                    for g in range(G):
                        pe.wait_ge(at_nrm, g + 1)
                        for b in range(3):
                            if b < 2:
                                bank = ps[3 * g + b]
                                for q in range(4):
                                    mm = pe.transpose(bank[:, q * P:(q + 1) * P],
                                                      qkv[:, g, b * 512 + q * P:b * 512 + (q + 1) * P], ident)
                            else:
                                bank = ps[3 * g + 2]
                                for j in range(2):
                                    mm = pe.transpose(bank[:, j * P:(j + 1) * P],
                                                      qkv[:, g, D + j * P:D + (j + 1) * P], ident)
                            mm.then_inc(at_tr, 1)
                    pe.wait_ge(at_trc, 7)

                    def at_scores(i):
                        g, j = divmod(i, NKV)
                        keys = T if g == 0 else 2 * T
                        k0 = 0 if g == 0 else T
                        o = HD * (j % 2)
                        bk = 2 * (i % 2)
                        if i >= 2:
                            pe.wait_ge(at_exp, i - 1)
                        for q in range(QG):
                            mm = pe.matmul(ps[bk + q // 2][:, (q % 2) * 256:(q % 2) * 256 + keys],
                                           qTt[o:o + HD, (j // 2) * QG + q, g * T:(g + 1) * T],
                                           kTt[o:o + HD, j // 2, k0:k0 + keys], start=True, stop=True)
                        mm.then_inc(at_s, 1)

                    def at_values(i):
                        g, j = divmod(i, NKV)
                        nk = 1 if g == 0 else 2
                        pe.wait_ge(at_exp, i + 1)
                        for kk in range(nk):
                            for q in range(QG):
                                mm = pe.transpose(ps[4 + kk][:, q * T:(q + 1) * T],
                                                  prob[:, i % 2, q, kk * T:(kk + 1) * T], ident)
                        mm.then_inc(at_pt, 1)
                        pe.wait_ge(at_ptc, i + 1)
                        if i >= 2:
                            pe.wait_ge(at_on, i - 1)
                        for q in range(QG):
                            for kk in range(nk):
                                v = (qkv[:, g, (NH + NKV + j) * HD:(NH + NKV + j + 1) * HD] if kk == 0
                                     else vctx[:, j * HD:(j + 1) * HD])
                                mm = pe.matmul(ps[6 + i % 2][:, q * HD:(q + 1) * HD],
                                               probT[:, kk, q * T:(q + 1) * T], v,
                                               start=(kk == 0), stop=(kk == nk - 1))
                        mm.then_inc(at_o, 1)

                    for i in range(G * NKV + 1):
                        if i < G * NKV:
                            at_scores(i)
                        if i >= 1:
                            at_values(i - 1)
                    pe.wait_ge(at_on, G * NKV)
                    for b in range(4):
                        for h in range(2):
                            for g in range(G):
                                mm = pe.transpose(
                                    ps[b][:, (2 * h + g) * T:(2 * h + g + 1) * T],
                                    otok[:, g, :].rearrange("p (m q) -> p q m", q=KC)[:, 2 * b + h, :], ident)
                        mm.then_inc(at_ot, 1)
                    project(wo, oT, at_otc, 4, ld_wo)

                sum_squares(3 if l == 0 else 5, 7)
                pe.wait_ge(h_ready, 2 * l + 2)
                for g in range(G):
                    for k in range(KC):
                        mm = pe.matmul(ps[7][:, g * NE:(g + 1) * NE], hT[:, k, g * T:(g + 1) * T], rw[:, l, k, :],
                                       start=(k == 0), stop=(k == KC - 1))
                mm.then_inc(rt_logits, 1)
                for g in range(G):
                    for h in range(2):
                        for k in range(4):
                            mm = pe.transpose(ps[2 * g + h][:, k * P:(k + 1) * P],
                                              hT[:, 4 * h + k, g * T:(g + 1) * T], ident)
                        mm.then_inc(ht_tr, 1)
                pe.wait_ge(ld_sh, 48 * (l + 1))
                for i in range(4):
                    w = (gate_of(shw) if i < 2 else up_of(shw)).rearrange("p k (m j) -> p k j m", j=FC)
                    for k in range(KC):
                        mm = pe.matmul(ps[4 + i // 2][:, (i % 2) * TT:(i % 2 + 1) * TT], w[:, k, i % 2, :],
                                       hT[:, k, :], start=(k == 0), stop=(k == KC - 1))
                mm.then_inc(sh_gu, 1)
                pe.wait_ge(rt_sel, l + 1)
                pe.matmul(ps[7][:, 0:NE], ubf[:, 0, :], selb[:, 0, :], start=True, stop=True)
                pe.matmul(ps[7][:, NE:2 * NE], ubf[:, 1, :], selb[:, 0, :], start=True, stop=False)
                pe.matmul(ps[7][:, NE:2 * NE], ubf[:, 0, :], selb[:, 1, :], start=False, stop=True)
                for g in range(G):
                    mm = pe.matmul(ps[7][0:NE, 2 * NE:2 * NE + 2], selb[:, g, :], ubf[:, 1, 0:2],
                                   start=(g == 0), stop=(g == G - 1))
                mm.then_inc(rt_rank, 1)
                pe.wait_ge(rt_nov, l + 1)
                pe.matmul(ps[7][:, 0:NE], novb[:, :], ubf[0:NE, 0, 0:NE], start=True, stop=True)
                pe.matmul(ps[7][0:NE, NE:NE + 2], ubf[0:NE, 0, 0:NE], novb[:, 0:2], start=True, stop=True)
                mm = pe.matmul(ps[7][0:1, 2 * NE:2 * NE + 2], ubf[0:NE, 1, 0:1], novb[:, 0:2], start=True, stop=True)
                mm.then_inc(rt_pos, 1)
                pe.wait_ge(rt_list, l + 1)
                pe.matmul(ps[7][0:1, 0:MAXOVF], ubf[0:NE, 1, 0:1], ovl[:, :],
                          start=True, stop=True).then_inc(rt_tab, 1)

                pe.wait_ge(sh_hid, l + 1)
                pe.wait_ge(rt_table, l + 1)
                pe.wait_ge(zeroed, l + 1)
                for b in range(4):
                    pe.matmul(acc[b][:, :], zer, cst[:, 0:512], start=True, stop=False, skip_group_check=True)
                for k in range(KC):
                    for j in range(FC):
                        mm = pe.matmul(acc[k // 2][:, (k % 2) * TT:(k % 2 + 1) * TT],
                                       down_of(shw)[:, j, :].rearrange("p (m q) -> p q m", q=KC)[:, k, :],
                                       shh[:, 2 + j, :], start=False, stop=False, skip_group_check=True)
                mm.then_inc(sh_done, 1)

                def gather(i, half):
                    for kk in range(4):
                        for n, (g, part) in enumerate((g, part) for g in range(G) for part in range(3)):
                            mm = pe.matmul(PG[:, kk * P:(kk + 1) * P], hbf[:, part, g, 4 * half + kk, :],
                                           gbf[:, g, :], start=(n == 0), stop=(n == 2 * 3 - 1))
                    mm.then_inc(pe_gather[l], 1)

                def gate_up(i, par):
                    pe.wait_ge(act_xg[l], 2 * i + 2)
                    for b in range(2):
                        pe.wait_ge(ld_gu[l][2 * par + b], 16 * (i - par) + 32)
                    for h, part in enumerate((gate_of, up_of)):
                        for k in range(KC):
                            for b in range(2):
                                mm = pe.matmul(PGU[64 * b:64 * b + 64, h * DE:(h + 1) * DE],
                                               xg[:, k, 64 * b:64 * b + 64], part(ring[:, 2 * par + b, :])[:, k, :],
                                               start=(k == 0), stop=(k == KC - 1))
                    mm.then_inc(pe_gu[l], 1)

                def combine_t(i):
                    pe.wait_ge(dve_gw[l], i + 1)
                    for g in range(G):
                        mm = pe.transpose(PT[:, 256 + g * T:256 + (g + 1) * T], gw[:, g, :], ident)
                    mm.then_inc(pe_ct[l], 1)

                def hidden_t(i):
                    pe.wait_ge(dve_h[l], i + 1)
                    pe.wait_ge(dve_c[l], i + 1)
                    for j in range(FC):
                        mm = pe.transpose(PT[:, j * P:(j + 1) * P],
                                          hid.rearrange("p (m j) -> p j m", j=FC)[:, j, :], ident)
                    mm.then_inc(pe_ht[l], 1)

                def down(i, par):
                    pe.wait_ge(dve_ht[l], i + 1)
                    for b in range(2):
                        pe.wait_ge(ld_dn[l][2 * par + b], 8 * (i - par) + 16)
                    for n, bank in ((1, PGU), (0, PY)):
                        for j in range(FC):
                            for b in range(2):
                                mm = pe.matmul(bank[64 * b:64 * b + 64, :], hidT[:, j, 64 * b:64 * b + 64],
                                               down_of(ring[:, 2 * par + b, :])[:, j, n * 512:(n + 1) * 512],
                                               start=(j == 0), stop=(j == FC - 1))
                        mm.then_inc(pe_dn[l], 1)

                def combine(i, par):
                    pe.wait_ge(dve_y[l], i + 1)
                    pe.wait_ge(act_y[l], i + 1)
                    for k in range(KC):
                        mm = pe.matmul(acc[k // 2][:, (k % 2) * TT:(k % 2 + 1) * TT], ysb[:, k, :], comb[:, par, :],
                                       start=False, stop=False, skip_group_check=True)
                    mm.then_inc(pe_comb[l], 1)

                def pair(i, par, first=False, last=False):
                    if not first:
                        pe.wait_ge(act_y[l], i)
                    gate_up(i, par)
                    combine_t(i)
                    if not last:
                        pe.wait_ge(dve_g[l], i + 2)
                        gather(i + 1, 0)
                    if not first:
                        combine(i - 1, 1 - par)
                    hidden_t(i)
                    if not last:
                        pe.wait_ge(act_xg[l], 2 * i + 3)
                        gather(i + 1, 1)
                    down(i, par)

                pe.wait_ge(ht_done, l + 1)
                pe.wait_ge(dve_g[l], 1)
                gather(0, 0)
                pe.wait_ge(act_xg[l], 1)
                gather(0, 1)
                pair(0, 0, first=True)
                pair(1, 1)
                with pe.Fori(1, PAIRS // 2 - 1) as it:
                    for par in range(2):
                        pair(2 * it + par, par)
                pair(PAIRS - 2, 0)
                pair(PAIRS - 1, 1, last=True)
                combine(PAIRS - 1, 1)
                nov = pe.value_load(table[0:1, 0:1], min_val=0, max_val=MAXOVF)
                with pe.Fori(0, OVF_PAIRS // 2) as it:
                    for par in range(2):
                        with pe.If(nov > 4 * it + 2 * par):
                            i = 2 * it + par + PAIRS
                            pe.wait_ge(dve_g[l], i + 1)
                            gather(i, 0)
                            pe.wait_ge(act_xg[l], 2 * i + 1)
                            gather(i, 1)
                            gate_up(i, par)
                            combine_t(i)
                            hidden_t(i)
                            down(i, par)
                            combine(i, par)
                pe.matmul(PG[:, 0:2], zer, ones[:, 0:2], start=True, stop=True).then_inc(moe_done, 1)

            pe.wait_ge(y_ready, L * KC)
            for g in range(G):
                for h in range(2):
                    for k in range(4):
                        mm = pe.transpose(ps[2 * g + h][:, k * P:(k + 1) * P],
                                          yT[:, 4 * h + k, g * T:(g + 1) * T], ident)
                    mm.then_inc(y_tr, 1)

        @block.scalar
        def _(act):
            steps = [0]

            def step(ins):
                steps[0] += 1
                ins.then_inc(act_step, 1)
                act.wait_ge(act_step, steps[0])

            act.wait_ge(ld_cond, 32)
            act.wait_ge(cond_zero, 1)
            act.activation(scT[:, :, 0:2], cT[:, :, :].rearrange("p c k -> p k c"), ACT.Silu).then_inc(cond_ready, 1)
            act.wait_ge(ld_small, 16 * N_SMALL)
            for b in range(4):
                act.wait_ge(x_tr, b + 1)
                act.activation(yT[:, 2 * b:2 * b + 2, :].rearrange("p k t -> p (k t)"), ps[3 + b][:, :],
                               ACT.Copy).then_inc(x_in, 1)

            def ada_copy(l):
                act.wait_ge(ada_used, KC * (l + 1))
                if l == 1:
                    act.wait_ge(cv_u, KC)
                for b in range(3):
                    act.activation(arow[:, b, :], ps[b][:, :], ACT.Copy).then_inc(ada_rows, 1)

            def squares(src, n):
                act.activation(sq, src, ACT.Square).then_inc(sq_ready, 1)
                act.wait_ge(ss_ready, n)
                act.activation(rstd[:, :], ps[7][:, 0:TT], ACT.Sqrt, bias=epsc[:, 0:1], scale=1.0 / D
                               ).then_inc(root_ready, 1)

            ada_copy(0)
            act.wait_ge(x_in, 4)
            for l in range(L):
                if l == 1:
                    act.wait_ge(y_ready, KC)
                squares(yT[:, :, :], 1 if l == 0 else 4)
                if l == 0:
                    for cc in range(KC):
                        act.wait_ge(cv_u, cc + 1)
                        if cc >= 2:
                            act.wait_ge(cv_in, cc - 1)
                        act.activation(sgt[:, cc % 2, :], ps[3 + cc % 4][:, TT:2 * TT], ACT.Sigmoid,
                                       bias=b1c[:, 1, cc:cc + 1]).then_inc(cv_gate, 1)
                    ada_copy(1)
                    act.wait_ge(cv_out, KC)
                    squares(dwo, 2)
                    for cc in range(KC):
                        act.wait_ge(cn_scaled, 1)
                        act.activation(dwo[:, cc, :], dwo[:, cc, :], ACT.Silu, scale=cvec[:, 1, cc:cc + 1]
                                       ).then_inc(cn_ready, 1)
                    for k in range(KC):
                        act.wait_ge(pj_out, k // 2 + 1)
                        if k >= 2:
                            act.wait_ge(pj_done, k - 1)
                        act.activation(tmp2[:, k % 2, :], ps[3 + k // 2][:, (k % 2) * TT:(k % 2 + 1) * TT],
                                       ACT.Identity, bias=cvec[:, 2, k:k + 1]).then_inc(pj_bias, 1)
                else:
                    for i in range(6):
                        act.wait_ge(at_qkv, i + 1)
                        g, n = divmod(i, 3)
                        dst, src = qkv[:, g, n * 512:(n + 1) * 512], ps[i][:, :]
                        if n < 2:
                            dst = dst.rearrange("p (q o d) -> p q o d", o=2, q=QG)
                            src = src.rearrange("p (o q d) -> p q o d", o=2, q=QG)
                        ins = act.activation(dst, src, ACT.Copy)
                        if n == 2:
                            ins.then_inc(at_copied, 1)
                    for g in range(G):
                        act.wait_ge(at_qk, g + 1)
                        act.activation(stat[:, 20 * g:20 * g + 20], stat[:, 20 * g:20 * g + 20], ACT.Sqrt,
                                       bias=epsc[:, 0:1], scale=1.0 / HD).then_inc(at_root, 1)
                    for i in range(7):
                        act.wait_ge(at_tr, i + 1)
                        if i == 0:
                            src = ps[6][:, 0:256].rearrange("p (c t) -> p c t", c=2)
                            act.activation(kTt[:, :, 2 * T:3 * T], src, ACT.Copy).then_inc(at_trc, 1)
                            continue
                        g, b = divmod(i - 1, 3)
                        if b < 2:
                            act.activation(qTt[:, 4 * b:4 * b + 4, g * T:(g + 1) * T],
                                           ps[3 * g + b][:, :].rearrange("p (c t) -> p c t", c=4), ACT.Copy
                                           ).then_inc(at_trc, 1)
                        else:
                            act.activation(kTt[:, :, g * T:(g + 1) * T],
                                           ps[3 * g + 2][:, 0:256].rearrange("p (c t) -> p c t", c=2), ACT.Copy
                                           ).then_inc(at_trc, 1)

                    def exps(i):
                        g, j = divmod(i, NKV)
                        keys = T if g == 0 else 2 * T
                        act.wait_ge(at_max, i + 1)
                        if i >= 2:
                            act.wait_ge(at_pt, i - 1)
                        sk = stat[:, 112 + 4 * i:116 + 4 * i]
                        act.activation(sk, sk, ACT.Exp)
                        for q in range(QG):
                            m = 40 + 4 * i + q
                            ins = act.activation(prob[:, i % 2, q, 0:keys],
                                                 ps[2 * (i % 2) + q // 2][:, (q % 2) * 256:(q % 2) * 256 + keys],
                                                 ACT.Exp, bias=stat[:, m:m + 1], scale=HD ** -0.5,
                                                 accum_out=stat[:, 32 + m:32 + m + 1])
                        ins.then_inc(at_exp, 1)

                    for i in range(G * NKV):
                        exps(i)
                    for b in range(4):
                        act.wait_ge(at_ot, b + 1)
                        act.activation(oT[:, 2 * b:2 * b + 2, :].rearrange("p k t -> p (k t)"), ps[b][:, :],
                                       ACT.Copy).then_inc(at_otc, 1)
                act.wait_ge(h_ready, 2 * l + 1)
                act.wait_ge(pj_done, KC * (l + 1))
                squares(yT[:, :, :], 3 if l == 0 else 5)
                act.wait_ge(rt_logits, l + 1)
                act.activation(scores[:, :, :].rearrange("p g e -> p (g e)"), ps[7][:, 0:2 * NE], ACT.Sigmoid
                               ).then_inc(rt_score, 1)
                for i in range(4):
                    g, h = divmod(i, 2)
                    act.wait_ge(ht_tr, 4 * l + i + 1)
                    dst = hbf[:, 0, g, 4 * h:4 * h + 4, :].rearrange("p k m -> p (k m)")
                    act.activation(dst, ps[i][:, :], ACT.Copy).then_inc(ht_b1, 1)
                act.wait_ge(sh_gu, l + 1)
                act.activation(shh[:, 0:2, :].rearrange("p j t -> p (j t)"), ps[4][:, :], ACT.Silu).then_inc(sh_silu, 1)
                for i in range(4):
                    g, h = divmod(i, 2)
                    act.wait_ge(ht_r1, 4 * l + i + 1)
                    dst = hbf[:, 1, g, 4 * h:4 * h + 4, :].rearrange("p k m -> p (k m)")
                    act.activation(dst, ps[i][:, :], ACT.Copy).then_inc(ht_b2, 1)

                def gathered(i, half):
                    act.wait_ge(pe_gather[l], 2 * i + half + 1)
                    act.activation(xg[:, 4 * half:4 * half + 4, :].rearrange("p k s -> p (k s)"), PG[:, :], ACT.Copy
                                   ).then_inc(act_xg[l], 1)

                def silu(i):
                    act.wait_ge(pe_gu[l], i + 1)
                    act.activation(silu_h, PGU[:, 0:DE], ACT.Silu).then_inc(act_silu[l], 1)

                def y_upper(i):
                    act.wait_ge(pe_dn[l], 2 * i + 1)
                    act.activation(ysb[:, :, 64:128].rearrange("p k m -> p m k"),
                                   PGU[:, :].rearrange("p (m k) -> p m k", k=KC), ACT.Copy).then_inc(act_y[l], 1)

                def pair(i, last=False):
                    silu(i)
                    if not last:
                        gathered(i + 1, 0)
                        gathered(i + 1, 1)
                    y_upper(i)

                gathered(0, 0)
                gathered(0, 1)
                pair(0)
                pair(1)
                with act.Fori(1, PAIRS // 2 - 1) as it:
                    for par in range(2):
                        pair(2 * it + par)
                pair(PAIRS - 2)
                pair(PAIRS - 1, last=True)
                act.wait_ge(rt_table, l + 1)
                nov = act.value_load(table[0:1, 0:1], min_val=0, max_val=MAXOVF)
                with act.Fori(0, OVF_PAIRS // 2) as it:
                    for par in range(2):
                        with act.If(nov > 4 * it + 2 * par):
                            i = 2 * it + par + PAIRS
                            gathered(i, 0)
                            gathered(i, 1)
                            silu(i)
                            y_upper(i)

            for g in range(G):
                for h in range(2):
                    act.wait_ge(y_tr, 2 * g + h + 1)
                    dst = ytok[:, g, :].rearrange("p (m k) -> p k m", k=KC)[:, 4 * h:4 * h + 4, :]
                    act.activation(dst, ps[2 * g + h][:, :].rearrange("p (k m) -> p k m", k=4), ACT.Copy
                                   ).then_inc(y_out, 1)

        @block.vector
        def _(dve):
            steps = [0]

            def step(ins):
                steps[0] += 1
                ins.then_inc(dve_step, 1)
                dve.wait_ge(dve_step, steps[0])

            dve.memset(epsc[:, :], EPS)
            dve.memset(scT[:, :, 2:32], 0.0).then_inc(cond_zero, 1)
            dve.wait_ge(ld_const, 16)
            dve.tensor_copy(ubf[:, 0, :], cst[:, C_U:C_U + P])
            dve.tensor_copy(ubf[:, 1, :], ones).then_inc(bf_const, 1)
            dve.wait_ge(ld_small, 16 * N_SMALL)

            def ada_finish(l):
                for b in range(3):
                    dve.wait_ge(ada_cols, 3 * l + b + 1)
                    for cd in range(2):
                        src = ps[b][:, :].rearrange("p (q j r) -> p j q r", q=4, j=4)[:, :, :, cd]
                        ins = dve.tensor_tensor(
                            mod[:, l, cd, 16 * b:16 * b + 16].rearrange("p (j q) -> p j q", j=4), src,
                            adab[:, l, 2 * b:2 * b + 2, :].rearrange("p s (j q) -> p (s j) q", j=2), ALU.add)
                step(ins)
                for which in range(2):
                    for cd in range(2):
                        s = 1 + 3 * which
                        ins = dve.scalar_tensor_tensor(modA[:, l, which, cd, :], mod[:, l, cd, s * KC:(s + 1) * KC],
                                                       1.0, gains[:, l, which, :], ALU.add, ALU.mult)
                ins.then_inc(mod_ready, 1)

            def normalise(l, which):
                dve.wait_ge(mod_ready, l + 1)
                dve.wait_ge(root_ready, norms[0] + 1)
                norms[0] += 1
                step(dve.reciprocal(rstd[:, :], rstd[:, :]))
                step(dve.tensor_tensor(hT[:, :, :], yT[:, :, :], rstd[:, None, :].to_broadcast([P, KC, TT]), ALU.mult))
                for g in range(G):
                    for k in range(KC):
                        v = hT[:, k, g * T:(g + 1) * T]
                        ins = dve.tensor_scalar(v, v, modA[:, l, which, g, k:k + 1],
                                                mod[:, l, g, 3 * which * KC + k:3 * which * KC + k + 1],
                                                ALU.mult, ALU.add)
                ins.then_inc(h_ready, 1)

            norms = [0]
            dve.wait_ge(x_in, 4)
            ada_finish(0)
            for l in range(L):
                normalise(l, 0)
                if l == 0:
                    dve.memset(upad[:, :, :, 0:PAD], 0.0)
                    step(dve.memset(upad[:, :, :, PAD + T:], 0.0))
                    for cc in range(KC):
                        dve.wait_ge(cv_gate, cc + 1)
                        dve.scalar_tensor_tensor(
                            upad[:, cc, :, PAD:PAD + T], ps[3 + cc % 4][:, 0:TT].rearrange("p (g t) -> p g t", g=G),
                            b1c[:, 0, cc:cc + 1], sgt[:, cc % 2, :].rearrange("p (g t) -> p g t", g=G),
                            ALU.add, ALU.mult).then_inc(cv_in, 1)
                        dve.wait_ge(cv_in, cc + 1)
                        o = dwo[:, cc, :].rearrange("p (g t) -> p g t", g=G)
                        ins = dve.tensor_scalar(o, upad[:, cc, :, 0:T], dwc[:, 0, cc:cc + 1], cvec[:, 0, cc:cc + 1],
                                                ALU.mult, ALU.add)
                        for j in range(1, TAPS):
                            step(ins)
                            ins = dve.scalar_tensor_tensor(o, upad[:, cc, :, j:j + T], dwc[:, j, cc:cc + 1], o,
                                                           ALU.mult, ALU.add)
                        ins.then_inc(cv_out, 1)
                    ada_finish(1)
                    dve.wait_ge(root_ready, 2)
                    norms[0] += 1
                    step(dve.reciprocal(rstd[:, :], rstd[:, :]))
                    dve.tensor_tensor(dwo, dwo, rstd[:, None, :].to_broadcast([P, KC, TT]), ALU.mult
                                      ).then_inc(cn_scaled, 1)
                    for k in range(KC):
                        dve.wait_ge(pj_bias, k + 1)
                        for g in range(G):
                            v = yT[:, k, g * T:(g + 1) * T]
                            ins = dve.scalar_tensor_tensor(v, tmp2[:, k % 2, g * T:(g + 1) * T],
                                                           mod[:, l, g, 2 * KC + k:2 * KC + k + 1], v,
                                                           ALU.mult, ALU.add)
                        ins.then_inc(pj_done, 1)
                else:
                    nqk = NH + NKV
                    for g in range(G):
                        dve.wait_ge(at_copied, g + 1)
                        v = qkv[:, g, 0:nqk * HD]
                        v3 = v.rearrange("p (h d) -> p h d", d=HD)
                        st = stat[:, nqk * g:nqk * (g + 1)]
                        step(dve.tensor_tensor(asq[:, g, :], v, v, ALU.mult))
                        dve.tensor_reduce(st, asq[:, g, :].rearrange("p (h d) -> p h d", d=HD), AX_X, ALU.add
                                          ).then_inc(at_qk, 1)
                        dve.wait_ge(at_root, g + 1)
                        step(dve.reciprocal(st, st))
                        step(dve.tensor_tensor(v3, v3, st[:, :, None].to_broadcast([P, nqk, HD]), ALU.mult))
                        dve.tensor_tensor(v3[:, 0:NH, :], v3[:, 0:NH, :],
                                          qkn[:, 0:1, :].to_broadcast([P, NH, HD]), ALU.mult)
                        ins = dve.tensor_tensor(v3[:, NH:, :], v3[:, NH:, :],
                                                qkn[:, 1:2, :].to_broadcast([P, NKV, HD]), ALU.mult)
                        if g == 1:
                            step(ins)
                            r = v.rearrange("p (h r s d) -> p h r s d", r=2, s=2, d=HD // 4)
                            a2 = asq[:, 0, :].rearrange("p (h r s d) -> p h r s d", r=2, s=2, d=HD // 4)
                            b2 = asq[:, 1, :].rearrange("p (h r s d) -> p h r s d", r=2, s=2, d=HD // 4)
                            for ax in range(2):
                                cs = cosT[:, None, 16 * ax:16 * ax + 16].to_broadcast([P, nqk, 16])
                                sn = sinT[:, None, 16 * ax:16 * ax + 16].to_broadcast([P, nqk, 16])
                                for s in range(2):
                                    dve.tensor_tensor(a2[:, :, ax, s], r[:, :, ax, s], cs, ALU.mult)
                                    ins = dve.tensor_tensor(b2[:, :, ax, s], r[:, :, ax, 1 - s], sn, ALU.mult)
                            step(ins)
                            for ax in range(2):
                                dve.tensor_tensor(r[:, :, ax, 0], a2[:, :, ax, 0], b2[:, :, ax, 0], ALU.subtract)
                                ins = dve.tensor_tensor(r[:, :, ax, 1], a2[:, :, ax, 1], b2[:, :, ax, 1], ALU.add)
                        ins.then_inc(at_nrm, 1)

                    def maxima(i):
                        g, j = divmod(i, NKV)
                        keys = T if g == 0 else 2 * T
                        dve.wait_ge(at_s, i + 1)
                        mx = stat[:, 104 + 4 * (i % 2):108 + 4 * (i % 2)]
                        for b in range(2):
                            ins = dve.tensor_reduce(
                                mx[:, 2 * b:2 * b + 2],
                                ps[2 * (i % 2) + b][:, :].rearrange("p (h s) -> p h s", h=2)[:, :, 0:keys],
                                AX_X, ALU.max)
                        step(ins)
                        step(dve.scalar_tensor_tensor(mx, mx, HD ** -0.5, sinkb[:, 4 * j:4 * j + 4],
                                                      ALU.mult, ALU.max))
                        dve.tensor_tensor(stat[:, 112 + 4 * i:116 + 4 * i], sinkb[:, 4 * j:4 * j + 4], mx, ALU.subtract)
                        dve.tensor_scalar(stat[:, 40 + 4 * i:44 + 4 * i], mx, -1.0, None, ALU.mult
                                          ).then_inc(at_max, 1)

                    def outputs(i):
                        g, j = divmod(i, NKV)
                        nk = 1 if g == 0 else 2
                        dve.wait_ge(at_pt, i + 1)
                        for kk in range(nk):
                            ins = dve.tensor_copy(probT[:, kk, :], ps[4 + kk][:, :])
                        ins.then_inc(at_ptc, 1)
                        dve.wait_ge(at_o, i + 1)
                        step(dve.tensor_tensor(stat[:, 72 + 4 * i:76 + 4 * i], stat[:, 72 + 4 * i:76 + 4 * i],
                                               stat[:, 112 + 4 * i:116 + 4 * i], ALU.add))
                        step(dve.reciprocal(stat[:, 72 + 4 * i:76 + 4 * i], stat[:, 72 + 4 * i:76 + 4 * i]))
                        dve.tensor_tensor(
                            otok[:, g, 4 * j * HD:4 * (j + 1) * HD].rearrange("p (h d) -> p h d", h=QG),
                            ps[6 + i % 2][:, 0:QG * HD].rearrange("p (h d) -> p h d", h=QG),
                            stat[:, 72 + 4 * i:76 + 4 * i, None].to_broadcast([P, QG, HD]), ALU.mult
                        ).then_inc(at_on, 1)

                    for i in range(G * NKV + 1):
                        if i < G * NKV:
                            maxima(i)
                        if i >= 1:
                            outputs(i - 1)
                    for k in range(KC):
                        dve.wait_ge(pj_out, 4 + k // 2 + 1)
                        for g in range(G):
                            v = yT[:, k, g * T:(g + 1) * T]
                            ins = dve.scalar_tensor_tensor(
                                v, ps[3 + k // 2][:, (k % 2) * TT + g * T:(k % 2) * TT + (g + 1) * T],
                                mod[:, l, g, 2 * KC + k:2 * KC + k + 1], v, ALU.mult, ALU.add)
                        ins.then_inc(pj_done, 1)

                normalise(l, 1)
                dve.wait_ge(rt_score, l + 1)
                step(dve.tensor_tensor(choice[:, :, :], scores[:, :, :],
                                       rbias[:, l:l + 1, :].to_broadcast([P, G, NE]), ALU.add))
                for g in range(G):
                    for r in range(NGRP):
                        ins = dve.max(top8[:, g, r, :], choice[:, g, r * EPG:(r + 1) * EPG])
                step(ins)
                step(dve.tensor_tensor(gsc[:, :, :], top8[:, :, :, 0], top8[:, :, :, 1], ALU.add))
                for g in range(G):
                    mine = gsc[:, g, :, None].to_broadcast([P, NGRP, NGRP])
                    other = gsc[:, g, None, :].to_broadcast([P, NGRP, NGRP])
                    dve.tensor_tensor(gcmp[:, g], other, mine, ALU.is_gt)
                    ins = dve.tensor_tensor(gcmp2[:, g], other, mine, ALU.is_equal)
                step(ins)
                for g in range(G):
                    ins = dve.tensor_tensor(gcmp2[:, g], gcmp2[:, g], tri.rearrange("p (a b) -> p a b", a=NGRP), ALU.mult)
                step(ins)
                step(dve.tensor_tensor(gcmp[:, :, :, :], gcmp[:, :, :, :], gcmp2[:, :, :, :], ALU.add))
                step(dve.tensor_reduce(gsc[:, :, :], gcmp[:, :, :, :], AX_X, ALU.add))
                step(dve.tensor_scalar(gsc[:, :, :], gsc[:, :, :], TOPG - 0.5, None, ALU.is_lt))
                gm = [gsc[:, g, :, None].to_broadcast([P, NGRP, EPG]) for g in range(G)]
                for g in range(G):
                    ch = choice[:, g, :].rearrange("p (a b) -> p a b", a=NGRP)
                    dve.tensor_tensor(ch, ch, gm[g], ALU.mult)
                    ins = dve.tensor_scalar(sel[:, g, :].rearrange("p (a b) -> p a b", a=NGRP), gm[g], 1.0, BIG,
                                            ALU.subtract, ALU.mult)
                step(ins)
                step(dve.tensor_tensor(choice[:, :, :], choice[:, :, :], sel[:, :, :], ALU.add))
                for g in range(G):
                    ins = dve.max(top8[:, g, 0, :], choice[:, g, :])
                step(ins)
                for g in range(G):
                    ins = dve.match_replace(sel[:, g, :], top8[:, g, 0, :], choice[:, g, :], -2 * BIG)
                step(ins)
                step(dve.tensor_tensor(sel[:, :, :], sel[:, :, :], choice[:, :, :], ALU.not_equal))
                dve.tensor_copy(selb[:, :, :], sel[:, :, :]).then_inc(rt_sel, 1)
                step(dve.tensor_tensor(wt[:, :, :], scores[:, :, :], sel[:, :, :], ALU.mult))
                step(dve.tensor_reduce(wsum[:, :, 0], wt[:, :, :], AX_X, ALU.add))
                step(dve.reciprocal(wsum[:, :, 1], wsum[:, :, 0]))
                for g in range(G):
                    ins = dve.tensor_scalar(wt[:, g, :], wt[:, g, :], wsum[:, g, 1:2], ROUTED_SCALE,
                                            ALU.mult, ALU.mult)
                step(ins)
                dve.wait_ge(rt_rank, l + 1)
                step(dve.scalar_tensor_tensor(rank[:, :, :].rearrange("p g e -> p (g e)"), ps[7][:, 0:2 * NE], 1.0,
                                              sel[:, :, :].rearrange("p g e -> p (g e)"), ALU.add, ALU.mult))
                dve.tensor_scalar(rank[:, :, :], rank[:, :, :], -1.0, None, ALU.add)
                step(dve.tensor_copy(novc[:, 0:1], ps[7][0:NE, 2 * NE:2 * NE + 1]))
                for n in range(3):
                    ins = dve.tensor_scalar(novc[:, 1 + n:2 + n], novc[:, 0:1], (n + 1) * SLOTS + 0.5, None, ALU.is_gt)
                step(ins)
                step(dve.tensor_tensor(novc[:, 4:5], novc[:, 1:2], novc[:, 2:3], ALU.add))
                step(dve.tensor_tensor(novc[:, 4:5], novc[:, 4:5], novc[:, 3:4], ALU.add))
                dve.tensor_scalar(novb[:, :], ones[0:NE, :], novc[:, 4:5], None, ALU.mult).then_inc(rt_nov, 1)
                dve.wait_ge(rt_pos, l + 1)
                step(dve.tensor_scalar(ovrank[:, 0, :], ps[7][:, 0:NE], 1.0, float(SLOTS), ALU.subtract, ALU.mult))
                step(dve.tensor_copy(ovrank[:, 1, :], ovrank[:, 0, :]))
                dve.tensor_tensor(ovrank[:, :, :], ovrank[:, :, :], rank[:, :, :], ALU.add).then_inc(dve_ov[l], 1)
                step(dve.tensor_tensor(endc[:, :], novc[:, 4:5], ps[7][0:NE, NE:NE + 1], ALU.add))
                dve.tensor_copy(table[0:1, 0:1], ps[7][0:1, 2 * NE:2 * NE + 1])
                dve.tensor_scalar(ovl[:, :], iota[0:NE, 0:MAXOVF], endc[:, 0:1], None, ALU.is_ge).then_inc(rt_list, 1)
                dve.wait_ge(rt_tab, l + 1)
                dve.tensor_scalar(table[0:1, 1:1 + MAXOVF], ps[7][0:1, 0:MAXOVF], NE - 1.0, None, ALU.min
                                  ).then_inc(rt_table, 1)
                for i in range(4):
                    g, h = divmod(i, 2)
                    dve.wait_ge(ht_b1, 4 * l + i + 1)
                    dve.tensor_tensor(ps[i][:, :], ps[i][:, :],
                                      hbf[:, 0, g, 4 * h:4 * h + 4, :].rearrange("p k m -> p (k m)"), ALU.subtract
                                      ).then_inc(ht_r1, 1)
                for i in range(4):
                    g, h = divmod(i, 2)
                    dve.wait_ge(ht_b2, 4 * l + i + 1)
                    ins = dve.tensor_tensor(hbf[:, 2, g, 4 * h:4 * h + 4, :].rearrange("p k m -> p (k m)"), ps[i][:, :],
                                            hbf[:, 1, g, 4 * h:4 * h + 4, :].rearrange("p k m -> p (k m)"),
                                            ALU.subtract)
                ins.then_inc(ht_done, 1)
                dve.wait_ge(sh_silu, l + 1)
                dve.tensor_tensor(shh[:, 2:4, :].rearrange("p j t -> p (j t)"),
                                  shh[:, 0:2, :].rearrange("p j t -> p (j t)"), ps[5][:, :], ALU.mult
                                  ).then_inc(sh_hid, 1)
                dve.memset(zer, 0.0).then_inc(zeroed, 1)

                def one_hot(i, ranks):
                    for g in range(G):
                        for b in range(2):
                            ins = dve.tensor_scalar(gbf[:, g, 64 * b:64 * b + 64], iota,
                                                    ranks(g, b), None, ALU.is_equal)
                    ins.then_inc(dve_g[l], 1)

                def weighted(i, ranks, weights):
                    for g in range(G):
                        for b in range(2):
                            ins = dve.tensor_scalar(gw[:, g, 64 * b:64 * b + 64], iota,
                                                    ranks(g, b), weights(g, b), ALU.is_equal, ALU.mult)
                    ins.then_inc(dve_gw[l], 1)

                def of_pair(i):
                    if type(i) is int:
                        return (lambda g, b: rank[:, g, 2 * i + b:2 * i + b + 1],
                                lambda g, b: wt[:, g, 2 * i + b:2 * i + b + 1])
                    return (lambda g, b: rank[:, g, bass.ds(2 * i + b, 1)],
                            lambda g, b: wt[:, g, bass.ds(2 * i + b, 1)])

                def combine_copy(i, par):
                    dve.wait_ge(pe_ct[l], i + 1)
                    dve.tensor_copy(comb[:, par, :], PT[:, 256:512]).then_inc(dve_c[l], 1)

                def hidden(i):
                    dve.wait_ge(act_silu[l], i + 1)
                    dve.tensor_tensor(hid, silu_h, PGU[:, DE:2 * DE], ALU.mult).then_inc(dve_h[l], 1)

                def hidden_copy(i):
                    dve.wait_ge(pe_ht[l], i + 1)
                    dve.tensor_copy(hidT.rearrange("p j s -> p (j s)"), PT[:, 0:256]).then_inc(dve_ht[l], 1)

                def y_lower(i):
                    dve.wait_ge(pe_dn[l], 2 * i + 2)
                    dve.tensor_copy(ysb[:, :, 0:64].rearrange("p k m -> p m k"),
                                    PY[:, :].rearrange("p (m k) -> p m k", k=KC)).then_inc(dve_y[l], 1)

                def pair(i, par, last=False):
                    if not last:
                        r, w = of_pair(i + 1)
                        one_hot(i + 1, r)
                    combine_copy(i, par)
                    if not last:
                        weighted(i + 1, r, w)
                    hidden(i)
                    hidden_copy(i)
                    y_lower(i)

                r, w = of_pair(0)
                one_hot(0, r)
                weighted(0, r, w)
                dve.wait_ge(pe_gather[l], 2)
                pair(0, 0)
                pair(1, 1)
                with dve.Fori(1, PAIRS // 2 - 1) as it:
                    for par in range(2):
                        pair(2 * it + par, par)
                pair(PAIRS - 2, 0)
                pair(PAIRS - 1, 1, last=True)
                dve.wait_ge(rt_table, l + 1)
                nov = dve.value_load(table[0:1, 0:1], min_val=0, max_val=MAXOVF)
                with dve.Fori(0, OVF_PAIRS // 2) as it:
                    for par in range(2):
                        with dve.If(nov > 4 * it + 2 * par):
                            i = 2 * it + par + PAIRS
                            j = 2 * it + par
                            e = [dve.value_load(table[0:1, bass.ds(2 * j + b + 1, 1)], min_val=0, max_val=NE - 1)
                                 for b in range(2)]
                            dve.wait_ge(dve_ov[l], 3 * j + 1)

                            for b in range(2):
                                for g in range(G):
                                    w_ins = dve.tensor_scalar(
                                        gw[:, g, 64 * b:64 * b + 64], iota, ovrank[:, g, bass.ds(e[b], 1)],
                                        wt[:, g, bass.ds(e[b], 1)], ALU.is_equal, ALU.mult)
                                    ins = dve.tensor_scalar(gbf[:, g, 64 * b:64 * b + 64], iota,
                                                            ovrank[:, g, bass.ds(e[b], 1)], None, ALU.is_equal)
                                if b == 0:
                                    ins.then_inc(dve_ov[l], 1)
                                    dve.wait_ge(dve_ov[l], 3 * j + 2)
                                else:
                                    w_ins.then_inc(dve_gw[l], 1)
                                    ins.then_inc(dve_g[l], 1)
                                    dve.wait_ge(dve_g[l], i + 1)
                                dve.tensor_scalar(ovrank[:, :, :], ovrank[:, :, :], -float(SLOTS), None, ALU.add
                                                  ).then_inc(dve_ov[l], 1)
                                dve.wait_ge(dve_ov[l], 3 * j + b + 3)
                            combine_copy(i, par)
                            hidden(i)
                            hidden_copy(i)
                            y_lower(i)
                dve.wait_ge(moe_done, l + 1)
                for k in range(KC):
                    for g in range(G):
                        v = yT[:, k, g * T:(g + 1) * T]
                        ins = dve.scalar_tensor_tensor(
                            v, acc[k // 2][:, (k % 2) * TT + g * T:(k % 2) * TT + (g + 1) * T],
                            mod[:, l, g, 5 * KC + k:5 * KC + k + 1], v, ALU.mult, ALU.add)
                    ins.then_inc(y_ready, 1)


def shape_constants():
    import numpy as np

    a = np.zeros((P, C_W), np.float32)
    a[:, C_ID:C_ID + P] = np.eye(P)
    a[:, C_ONE:C_ONE + P] = 1.0
    a[:, C_U:C_U + P] = np.triu(np.ones((P, P)), 1)
    a[:, C_IOTA:C_IOTA + 64] = np.arange(64)[None, :]
    a[:, C_TRI:C_TRI + 64] = np.tril(np.ones((8, 8)), -1).reshape(1, 64)
    inv = np.float32(10000.0) ** (-np.arange(16, dtype=np.float32) / np.float32(16))
    pos = np.arange(P)
    for ax, at in enumerate((pos // 64, pos % 64)):
        ang = at.astype(np.float32)[:, None] * inv[None, :].astype(np.float32)
        a[:, C_COS + 16 * ax:C_COS + 16 * ax + 16] = np.cos(ang)
        a[:, C_SIN + 16 * ax:C_SIN + 16 * ax + 16] = np.sin(ang)
    return a


_INS = ['x_prompt', 'x_sample', 'cache_k', 'cache_v', 'c', 'c_ctx', 'ada_w', 'ada_b', 'norm_mix', 'norm_ffn',
        'conv_w1', 'conv_b1', 'conv_dw', 'conv_dw_b', 'conv_norm', 'conv_w2', 'conv_b2',
        'attn_wqkv', 'attn_q_norm', 'attn_k_norm', 'attn_sink', 'attn_wo',
        'router_w', 'router_bias', 'exp_w_gate', 'exp_w_up', 'exp_w_down', 'sh_w_gate', 'sh_w_up', 'sh_w_down']
_OUTS = [(1, T, D), (1, T, D), (1, 1, T, NKV, HD), (1, 1, T, NKV, HD)]


def kernel(**inputs):
    import numpy as _np
    import concourse.bacc as _bacc
    from concourse import mybir as _mybir
    from concourse.bass_utils import run_bass_kernel_spmd as _run

    nc = _bacc.Bacc("TRN2", target_bir_lowering=False, num_devices=1)
    arrays, args = {}, []
    for name in _INS:
        a = _np.ascontiguousarray(inputs[name])
        arrays[f"in_{name}_dram"] = a
        args.append(nc.dram_tensor(f"in_{name}_dram", a.shape, _mybir.dt.from_np(a.dtype), kind="ExternalInput").ap())
    a = shape_constants()
    arrays["in_consts_dram"] = a
    args.append(nc.dram_tensor("in_consts_dram", a.shape, F32, kind="ExternalInput").ap())
    for i, shape in enumerate(_OUTS):
        args.append(nc.dram_tensor(f"out_{i}_dram", shape, F32, kind="ExternalOutput").ap())
    build_kernel(nc, *args)
    r = _run(nc, [arrays], core_ids=[0])
    return tuple(r.results[0][f"out_{i}_dram"] for i in range(len(_OUTS)))
```

```python
from contextlib import ExitStack

import concourse.bass as bass
from concourse import mybir

F32 = mybir.dt.float32
BF16 = mybir.dt.bfloat16
I32 = mybir.dt.int32
ALU = mybir.AluOpType
ACT = mybir.ActivationFunctionType
AX_X = mybir.AxisListType.X

P = 128
D = 1024
KC = D // P
T = 128
G = 2
TT = G * T
L = 2
NADA = 6
TAPS = 31
PAD = TAPS // 2
NH, NKV, HD = 16, 4, 64
QG = NH // NKV
QKVW = (NH + 2 * NKV) * HD
NE, NGRP, TOPG, TOPK = 64, 8, 4, 8
EPG = NE // NGRP
DE = 256
FC = DE // P
ROUTED_SCALE = 2.5
EPS = 1e-6
SLOTS = 64
PAIRS = NE // 2
MAXOVF = TT * TOPK // (SLOTS + 1) + 1
OVF_PAIRS = MAXOVF // 2
BIG = 1e30
EW = 3 * D * DE // P

N_LOOP = (PAIRS - 4) // 2

UNIT = 2 * D
N_UNITS = L * 3 * KC
EARLY = 4 * KC


def unit_slot(u):
    if u < EARLY:
        return u % 6
    return u - EARLY if u < EARLY + 6 else 4 + u % 2


def unit_before(u):
    return next((v for v in range(u - 1, -1, -1) if unit_slot(v) == unit_slot(u)), None)


def unit_loads(u):
    return sum(unit_slot(v) == unit_slot(u) for v in range(u + 1))


CONV_ORDER = [0, KC - 1] + list(range(1, KC - 1))
PE_CHUNK = KC - 1

C_ID, C_ONE, C_U, C_IOTA, C_TRI, C_COS, C_SIN = 0, 128, 256, 384, 448, 512, 576
C_W = 640


def build_kernel(nc, x_prompt, x_sample, cache_k, cache_v, c, c_ctx, ada_w, ada_b, norm_mix, norm_ffn,
                 conv_w1, conv_b1, conv_dw, conv_dw_b, conv_norm, conv_w2, conv_b2,
                 attn_wqkv, attn_q_norm, attn_k_norm, attn_sink, attn_wo,
                 router_w, router_bias, exp_w_gate, exp_w_up, exp_w_down,
                 sh_w_gate, sh_w_up, sh_w_down, consts, y_prompt, y_sample, new_k, new_v):
    with ExitStack() as ctx:
        def sb(name, shape, dt=F32):
            return ctx.enter_context(nc.sbuf_tensor(name, shape, dt))

        def sem(name):
            return ctx.enter_context(nc.semaphore(name))

        cst = sb("cst", [P, C_W])
        ident = cst[:, C_ID:C_ID + P]
        ones = cst[:, C_ONE:C_ONE + P]
        iota = cst[:, C_IOTA:C_IOTA + SLOTS]
        tri = cst[:, C_TRI:C_TRI + 64]
        cosT = cst[:, C_COS:C_COS + 32]
        sinT = cst[:, C_SIN:C_SIN + 32]
        ubf = sb("ubf", [P, 2, P], BF16)
        yT = sb("yT", [P, KC, TT])
        hT = sb("hT", [P, KC, TT])
        hbf = sb("hbf", [P, 3, G, KC, P], BF16)
        rstd = sb("rstd", [P, TT])
        epsc = sb("epsc", [P, 1])
        cT = sb("cT", [P, 2, KC])
        scT = sb("scT", [P, KC, 32])
        mod = sb("mod", [P, L, 2, NADA * KC])
        modA = sb("modA", [P, L, 2, 2, KC])
        adab = sb("adab", [P, L, NADA, KC])
        gains = sb("gains", [P, L, 2, KC])
        cch = sb("cch", [P, 4, KC])
        dwc = sb("dwc", [P, KC, TAPS])
        b2c = sb("b2c", [P, KC])
        qkn = sb("qkn", [P, 2, HD])
        sinkb = sb("sinkb", [P, NH])
        rbias = sb("rbias", [P, L, NE])
        rw = sb("rw", [P, L, KC, NE])
        scores = sb("scores", [P, G, NE])
        gsc = sb("gsc", [P, G, NGRP])
        sel = sb("sel", [P, G, NE])
        selb = sb("selb", [P, G, NE], BF16)
        wt = sb("wt", [P, G, NE])
        wsum = sb("wsum", [P, G, 2])
        rank = sb("rank", [P, G, NE])
        ovrank = sb("ovrank", [P, G, NE])
        novc = sb("novc", [NE, 8])
        novb = sb("novb", [NE, P], BF16)
        ovl = sb("ovl", [NE, MAXOVF], BF16)
        endc = sb("endc", [NE, 1])
        table = sb("table", [1, 1 + MAXOVF], I32)
        ring = sb("ring", [P, 4, EW])
        S = sb("S", [P, 12288])
        W = sb("W", [P, 4608])

        ring_f = ring[:, :, :].rearrange("p s n -> p (s n)")
        w1 = ring_f[:, 0:16384].rearrange("p (k n) -> p k n", k=KC)
        w2 = ring_f[:, 16384:24576].rearrange("p (k n) -> p k n", k=KC)
        ada = S[:, :].rearrange("p (s n) -> p s n", s=6)

        def diag(j):
            n0 = (j // KC % 2) * D + CONV_ORDER[j // (2 * KC)] * P
            return w1[:, j % KC, n0:n0 + P]

        wqkv = S[:, :].rearrange("p (k n) -> p k n", k=KC)
        wo = S[:, 0:8192].rearrange("p (k n) -> p k n", k=KC)
        shw = S[:, 0:EW]
        extra = [S[:, 0:EW], S[:, EW:2 * EW]]

        def gate_of(w):
            return w[:, 0:2048].rearrange("p (k f) -> p k f", k=KC)

        def up_of(w):
            return w[:, 2048:4096].rearrange("p (k f) -> p k f", k=KC)

        def gate_up_of(w):
            return w[:, 0:4096].rearrange("p (h k f) -> p k h f", h=2, k=KC)

        def down_of(w):
            return w[:, 4096:6144].rearrange("p (j n) -> p j n", j=FC)

        xg = W[:, 0:1024].rearrange("p (k s) -> p k s", k=KC)
        shh = W[:, 2688:3712].rearrange("p (j t) -> p j t", j=4)
        gbf = W[:, 1024:1152].bitcast(BF16).rearrange("p (g s) -> p g s", g=G)
        identb = W[:, 1152:1216].bitcast(BF16)
        wt3 = W[:, 1216:1408].bitcast(BF16).rearrange("p (g s e) -> p g s e", g=G, s=3)
        comb = W[:, 1408:1664].bitcast(BF16).rearrange("p (b t) -> p b t", b=2)
        silu_h = W[:, 1664:1920]
        hid = W[:, 1920:2176]
        hidT = W[:, 2176:2432].rearrange("p (j s) -> p j s", j=FC)
        y3 = W[:, 2432:3968].bitcast(BF16).rearrange("p (s k m) -> p s k m", s=3, k=KC)
        yrem = W[:, 3968:4480]
        wst = W[:, 4480:4486].bitcast(BF16).rearrange("p (g s b) -> p g s b", g=G, s=3)
        wslot = W[:, 4488:4490]
        choice = W[:, 1408:1536].rearrange("p (g e) -> p g e", g=G)
        top8 = W[:, 1536:1664].rearrange("p (g r n) -> p g r n", g=G, r=NGRP)
        gcmp = W[:, 1664:1792].rearrange("p (g r n) -> p g r n", g=G, r=NGRP)
        gcmp2 = W[:, 1792:1920].rearrange("p (g r n) -> p g r n", g=G, r=NGRP)
        upad = W[:, 0:KC * G * (T + 2 * PAD)].rearrange("p (c g t) -> p c g t", c=KC, g=G)
        dwo = W[:, 2560:4608].rearrange("p (c t) -> p c t", c=KC)
        dwrow = W[:, 2560:3584]
        crow = W[:, 3584:3712]
        hb_f = hbf[:, :, :, :, :].rearrange("p s g k m -> p (s g k m)").bitcast(F32)
        sq = hb_f[:, 0:2048].rearrange("p (k t) -> p k t", k=KC)
        sgt = hb_f[:, 2048:2560].rearrange("p (b t) -> p b t", b=2)
        tmp2 = sgt
        odd = hb_f[:, 2560:2816]
        arow = hT[:, 0:6, :].rearrange("p k t -> p (k t)").rearrange("p (b n) -> p b n", b=3)
        xtok = ring_f[:, 16384:16384 + 2048].rearrange("p (g n) -> p g n", g=G)
        ytok = ring_f[:, 0:2048].rearrange("p (g n) -> p g n", g=G)
        B0 = 2 * EW
        qkv = ring_f[:, B0:B0 + 3072].rearrange("p (g n) -> p g n", g=G)
        asq = ring_f[:, B0 + 3072:B0 + 5632].rearrange("p (g n) -> p g n", g=G)
        prob = ring_f[:, B0 + 3072:B0 + 5120].rearrange("p (b h s) -> p b h s", b=2, h=QG)
        otok = ring_f[:, B0 + 6912:B0 + 8960].rearrange("p (g n) -> p g n", g=G)
        oT = ring_f[:, B0 + 8960:B0 + 11008].rearrange("p (k t) -> p k t", k=KC)
        vctx = ring_f[:, B0 + 11008:B0 + 11264]
        kctx = ring_f[:, B0 + 11264:B0 + 11520]
        stat = ring_f[:, B0 + 11520:B0 + 11776]
        qTt = W[:, 0:2048].rearrange("p (c t) -> p c t", c=KC)
        kTt = W[:, 2048:2816].rearrange("p (c t) -> p c t", c=2)
        probT = hb_f[:, 0:1024].rearrange("p (b n) -> p b n", b=2)

        def half_of(y, h):
            return y[:, :, 64 - 64 * h:128 - 64 * h].rearrange("p k m -> p m k")

        ps = [ctx.enter_context(nc.psum_tensor(f"ps{i}", [P, 512], F32)) for i in range(8)]
        PG, PT, PGU, PY = ps[0], ps[1], ps[2], ps[3]
        CB = ps[3:7]
        AB = [ps[4], ps[5], ps[6], ps[3]]
        acc = ps[4:8]

        dve_step, act_step = sem("dve_step"), sem("act_step")
        ld_const, ld_x, ld_cond = sem("ld_const"), sem("ld_x"), sem("ld_cond")
        ld_mod0, ld_rows, ld_small = sem("ld_mod0"), sem("ld_rows"), sem("ld_small")
        rows_tr, rows_in = sem("rows_tr"), sem("rows_in")
        ld_ada = [sem(f"ld_ada{i}") for i in range(6)]
        ld_w1 = [sem(f"ld_w1_{i}") for i in range(KC)]
        ld_w2, ld_qkv, ld_kv, ld_wo = sem("ld_w2"), sem("ld_qkv"), sem("ld_kv"), sem("ld_wo")
        ld_sh = sem("ld_sh")
        stored = sem("stored")
        cond_ready, cond_zero = sem("cond_ready"), sem("cond_zero")
        ada_used, ada_rows, ada_cols, mod_ready = sem("ada_used"), sem("ada_rows"), sem("ada_cols"), sem("mod_ready")
        x_tr, x_in = sem("x_tr"), sem("x_in")
        sq_ready, ss_ready, root_ready = sem("sq_ready"), sem("ss_ready"), sem("root_ready")
        nr_ready, h_ready = sem("nr_ready"), [sem("h_ready_prompt"), sem("h_ready_latent")]
        cv_u, cv_gate, cv_in, cv_out = sem("cv_u"), sem("cv_gate"), sem("cv_in"), sem("cv_out")
        cv_diag, cv_pe, cv_pe_out = sem("cv_diag"), sem("cv_pe"), sem("cv_pe_out")
        cn_scaled, cn_ready = sem("cn_scaled"), sem("cn_ready")
        pj_out, pj_bias, pj_done = sem("pj_out"), sem("pj_bias"), sem("pj_done")
        at_qkv, at_copied, at_qk, at_root, at_nrm, at_tr, at_trc = (
            sem("at_qkv"), sem("at_copied"), sem("at_qk"), sem("at_root"), sem("at_nrm"), sem("at_tr"), sem("at_trc"))
        at_s, at_max, at_exp, at_pt, at_ptc, at_o, at_on, at_ot, at_otc = (
            sem("at_s"), sem("at_max"), sem("at_exp"), sem("at_pt"), sem("at_ptc"), sem("at_o"), sem("at_on"),
            sem("at_ot"), sem("at_otc"))
        rt_logits, rt_score, rt_sel, rt_rank, rt_nov, rt_pos, rt_list, rt_tab, rt_table = (
            sem("rt_logits"), sem("rt_score"), sem("rt_sel"), sem("rt_rank"), sem("rt_nov"), sem("rt_pos"),
            sem("rt_list"), sem("rt_tab"), sem("rt_table"))
        ht_tr, ht_b1, ht_r1, ht_b2, ht_done = (
            sem("ht_tr"), sem("ht_b1"), sem("ht_r1"), sem("ht_b2"), sem("ht_done"))
        sh_gu, sh_silu, sh_hid, sh_done = sem("sh_gu"), sem("sh_silu"), sem("sh_hid"), sem("sh_done")
        moe_done, y_ready = sem("moe_done"), sem("y_ready")
        y_tr, y_out = sem("y_tr"), sem("y_out")
        ld_gu = [[sem(f"ld_gu{l}_{s}") for s in range(4)] for l in range(L)]
        ld_dn = [[sem(f"ld_dn{l}_{s}") for s in range(4)] for l in range(L)]
        ld_gu_x = [[sem(f"ld_gu_x{l}_{b}") for b in range(2)] for l in range(L)]
        ld_dn_x = [[sem(f"ld_dn_x{l}_{b}") for b in range(2)] for l in range(L)]
        pe_gather = [sem(f"pe_gather{l}") for l in range(L)]
        pe_gu = [sem(f"pe_gu{l}") for l in range(L)]
        pe_ct = [sem(f"pe_ct{l}") for l in range(L)]
        pe_ht = [sem(f"pe_ht{l}") for l in range(L)]
        pe_dn = [sem(f"pe_dn{l}") for l in range(L)]
        act_xg = [sem(f"act_xg{l}") for l in range(L)]
        act_silu = [sem(f"act_silu{l}") for l in range(L)]
        act_y1 = [sem(f"act_y1_{l}") for l in range(L)]
        act_y2 = [sem(f"act_y2_{l}") for l in range(L)]
        dve_g = [sem(f"dve_g{l}") for l in range(L)]
        dve_rem = [sem(f"dve_rem{l}") for l in range(L)]
        dve_c = [sem(f"dve_c{l}") for l in range(L)]
        dve_h = [sem(f"dve_h{l}") for l in range(L)]
        dve_ht = [sem(f"dve_ht{l}") for l in range(L)]
        dve_y = [sem(f"dve_y{l}") for l in range(L)]
        dve_ov = [sem(f"dve_ov{l}") for l in range(L)]

        N_SMALL = 4 + 2 * L + 3

        block = ctx.enter_context(nc.Block())

        @block.sync
        def _(sp):
            def cols(v):
                return v.rearrange("(p k) -> p k", k=KC)

            sp.dma_start(cT[:, 0, :], cols(c_ctx)).then_inc(ld_cond, 16)
            sp.dma_start(cT[:, 1, :], cols(c[0])).then_inc(ld_cond, 16)
            sp.dma_start(cst[:, :], consts).then_inc(ld_const, 16)

            def load_ada(units):
                for u in units:
                    l, b, k = u // (3 * KC), u // KC % 3, u % KC
                    if unit_before(u) is not None:
                        sp.wait_ge(ada_used, unit_before(u) + 1)
                    rows = ada_w[l].rearrange("(p k) n -> k p n", k=KC)
                    sp.dma_start(ada[:, unit_slot(u), :], rows[k, :, b * UNIT:(b + 1) * UNIT]
                                 ).then_inc(ld_ada[unit_slot(u)], 16)

            def load_weights(l, e, w, part, loaded):
                if part == "gu":
                    sp.dma_start(w[:, 0:2048], exp_w_gate[l, e].rearrange("(p k) f -> p (k f)", k=KC)
                                 ).then_inc(loaded, 16)
                    sp.dma_start(w[:, 2048:4096], exp_w_up[l, e].rearrange("(p k) f -> p (k f)", k=KC)
                                 ).then_inc(loaded, 16)
                else:
                    sp.dma_start(w[:, 4096:6144], exp_w_down[l, e].rearrange("(p j) n -> p (j n)", j=FC)
                                 ).then_inc(loaded, 16)

            def load_expert(l, e, s, part):
                load_weights(l, e, ring[:, s, :], part, ld_gu[l][s] if part == "gu" else ld_dn[l][s])

            def load_extra(l, b):
                for part, loaded in (("gu", ld_gu_x), ("dn", ld_dn_x)):
                    load_weights(l, 4 + b, extra[b], part, loaded[l][b])

            def load_expert_at(l, e, s, part):
                w = ring[:, s, :]
                if part == "gu":
                    for o, src in ((0, exp_w_gate), (2048, exp_w_up)):
                        sp.dma_start(w[:, o:o + 2048],
                                     src[l, bass.ds(e, 1)].rearrange("e (p k) f -> (e p) (k f)", k=KC)
                                     ).then_inc(ld_gu[l][s], 16)
                else:
                    sp.dma_start(w[:, 4096:6144],
                                 exp_w_down[l, bass.ds(e, 1)].rearrange("e (p j) n -> (e p) (j n)", j=FC)
                                 ).then_inc(ld_dn[l][s], 16)

            def load_shared(l):
                sp.dma_start(shw[:, 0:2048], sh_w_gate[l].rearrange("(p k) f -> p (k f)", k=KC)).then_inc(ld_sh, 16)
                sp.dma_start(shw[:, 2048:4096], sh_w_up[l].rearrange("(p k) f -> p (k f)", k=KC)).then_inc(ld_sh, 16)
                sp.dma_start(shw[:, 4096:6144], sh_w_down[l].rearrange("(p j) n -> p (j n)", j=FC)
                             ).then_inc(ld_sh, 16)

            def biases(l):
                return ada_b[l].rearrange("(s p k) -> p s k", s=NADA, k=KC)

            sp.dma_start(xtok[:, 0, :], x_prompt[0]).then_inc(ld_x, 16)
            sp.dma_start(xtok[:, 1, :], x_sample[0]).then_inc(ld_x, 16)
            sp.dma_start(crow[0:2 * KC, :], conv_b1[0].rearrange("(c p) -> c p", p=P)).then_inc(ld_rows, 16)
            sp.dma_start(crow[2 * KC:3 * KC, :], conv_dw_b[0].rearrange("(c p) -> c p", p=P)).then_inc(ld_rows, 16)
            sp.dma_start(crow[3 * KC:4 * KC, :], conv_norm[0].rearrange("(c p) -> c p", p=P)).then_inc(ld_rows, 16)
            sp.dma_start(dwrow[0:TAPS, :], conv_dw[0]).then_inc(ld_rows, 16)
            load_ada(range(2))
            sp.dma_start(adab[:, 0], biases(0)).then_inc(ld_mod0, 16)
            sp.dma_start(gains[:, 0, 0], cols(norm_mix[0])).then_inc(ld_mod0, 16)
            sp.dma_start(gains[:, 0, 1], cols(norm_ffn[0])).then_inc(ld_mod0, 16)
            load_ada(range(2, KC))
            for cc in CONV_ORDER:
                for h in range(2):
                    n0 = h * D + cc * P
                    sp.dma_start(w1[:, :, n0:n0 + P],
                                 conv_w1[0].rearrange("(p k) n -> p k n", k=KC)[:, :, n0:n0 + P]
                                 ).then_inc(ld_w1[cc], 16)
            load_ada(range(KC, KC + 12))
            sp.wait_ge(x_tr, 4)
            sp.dma_start(w2, conv_w2[0].rearrange("(k p) n -> p k n", k=KC)).then_inc(ld_w2, 16)
            load_ada(range(KC + 12, EARLY))
            def load_small(dst, src):
                sp.dma_start(dst, src).then_inc(ld_small, 16)

            load_small(b2c[:, :], cols(conv_b2[0]))
            load_small(adab[:, 1], biases(1))
            load_small(gains[:, 1, 0], cols(norm_mix[1]))
            load_small(gains[:, 1, 1], cols(norm_ffn[1]))
            for l in range(L):
                load_small(rbias[:, l], router_bias[l:l + 1, :].to_broadcast([P, NE]))
                load_small(rw[:, l], router_w[l].rearrange("(p k) e -> p k e", k=KC))
            load_small(qkn[:, 0], attn_q_norm[0:1, :].to_broadcast([P, HD]))
            load_small(qkn[:, 1], attn_k_norm[0:1, :].to_broadcast([P, HD]))
            load_small(sinkb[:, :], attn_sink[0:1, :].to_broadcast([P, NH]))

            for l in range(L):
                if l == 0:
                    sp.wait_ge(cv_u, KC)
                    sp.wait_ge(cv_pe, 1)
                else:
                    sp.wait_ge(moe_done, 1)
                    sp.dma_start(kctx, cache_k[0, 0].rearrange("t h d -> t (h d)")).then_inc(ld_kv, 16)
                    sp.dma_start(vctx, cache_v[0, 0].rearrange("t h d -> t (h d)")).then_inc(ld_kv, 16)
                for s in range(2):
                    load_expert(l, s, s, "gu")
                for s in range(2):
                    load_expert(l, s, s, "dn")
                if l == 0:
                    sp.wait_ge(ada_used, EARLY)
                    load_shared(0)
                    sp.wait_ge(pj_out, 4)
                else:
                    sp.wait_ge(at_qkv, 6)
                    load_ada(range(EARLY, EARLY + 6))
                    sp.wait_ge(at_nrm, 1)
                    sp.wait_ge(at_copied, 1)
                    sp.dma_start(new_k[0, 0].rearrange("t h d -> t (h d)"),
                                 qkv[:, 0, NH * HD:(NH + NKV) * HD]).then_inc(stored, 16)
                    sp.dma_start(new_v[0, 0].rearrange("t h d -> t (h d)"),
                                 qkv[:, 0, (NH + NKV) * HD:QKVW]).then_inc(stored, 16)
                    load_ada(range(EARLY + 6, EARLY + 8))
                    sp.wait_ge(ada_used, EARLY + 4)
                    sp.dma_start(wo, attn_wo[0].rearrange("(p k) n -> p k n", k=KC)).then_inc(ld_wo, 16)
                    load_ada(range(EARLY + 8, N_UNITS))
                    sp.wait_ge(pj_out, 8)
                    load_shared(1)
                    sp.wait_ge(stored, 32)
                for s in range(2, 4):
                    load_expert(l, s, s, "gu")
                for s in range(2, 4):
                    load_expert(l, s, s, "dn")
                load_extra(l, 1)
                sp.wait_ge(sh_done, l + 1)
                load_extra(l, 0)

                def load_pair(i, half, gu_before, dn_before, load):
                    sp.wait_ge(pe_gu[l], gu_before)
                    for b in range(2):
                        load(l, 2 * i + b, 2 * half + b, "gu")
                    sp.wait_ge(pe_dn[l], dn_before)
                    for b in range(2):
                        load(l, 2 * i + b, 2 * half + b, "dn")

                load_pair(3, 0, 1, 2, load_expert)
                load_pair(4, 1, 2, 4, load_expert)
                with sp.Fori(1, N_LOOP) as it:
                    for half in range(2):
                        load_pair(2 * it + half + 3, half, 2 * it + half + 2, 4 * it + 2 * half + 4, load_expert_at)
                load_pair(PAIRS - 1, 0, PAIRS - 2, 2 * PAIRS - 4, load_expert)
                sp.wait_ge(rt_table, l + 1)
                nov = sp.value_load(table[0:1, 0:1], min_val=0, max_val=MAXOVF)
                def overflow_pair(it, half):
                    e = [sp.value_load(table[0:1, bass.ds(4 * it + 2 * half + b + 1, 1)],
                                       min_val=0, max_val=NE - 1) for b in range(2)]
                    sp.wait_ge(pe_gu[l], 2 * it + half + PAIRS - 1)
                    for b in range(2):
                        load_expert_at(l, e[b], 2 * (1 - half) + b, "gu")
                    sp.wait_ge(pe_dn[l], 4 * it + 2 * half + 2 * PAIRS - 2)
                    for b in range(2):
                        load_expert_at(l, e[b], 2 * (1 - half) + b, "dn")

                with sp.If(nov > 0):
                    overflow_pair(0, 0)
                    with sp.If(nov > 2):
                        overflow_pair(0, 1)
                        with sp.If(nov > 4):
                            with sp.Fori(1, OVF_PAIRS // 2) as it:
                                for half in range(2):
                                    with sp.If(nov > 4 * it + 2 * half):
                                        overflow_pair(it, half)
                if l == 0:
                    sp.wait_ge(pe_dn[0], 6)
                    sp.dma_start(wqkv, attn_wqkv[0].rearrange("(p k) n -> p k n", k=KC)).then_inc(ld_qkv, 16)
            for g, y in enumerate((y_prompt, y_sample)):
                sp.wait_ge(y_out, 2 * (g + 1))
                sp.dma_start(y[0], ytok[:, g, :]).then_inc(stored, 16)
            sp.wait_ge(stored, 64)

        @block.tensor
        def _(pe):
            def ada_products(units, bank):
                for u in units:
                    k, slot = u % KC, unit_slot(u)
                    pe.wait_ge(ld_ada[slot], 16 * unit_loads(u))
                    for j in range(4):
                        rhs = ada[:, slot, (j // 2) * D:(j // 2 + 1) * D].rearrange(
                            "p (m q) -> p q m", q=KC)[:, 4 * (j % 2):4 * (j % 2) + 4, :]
                        mm = pe.matmul(bank[32 * j:32 * j + 32, :].rearrange("p (q m) -> p q m", q=4),
                                       scT[:, k, :], rhs, start=(k == 0), stop=(k == KC - 1))
                    mm.then_inc(ada_used, 1)

            def ada_transposes(e, bank):
                pe.wait_ge(ada_rows, e + 1)
                for q in range(4):
                    mm = pe.transpose(bank[:, q * P:(q + 1) * P], arow[:, e % 3, q * P:(q + 1) * P], ident)
                mm.then_inc(ada_cols, 1)

            def sum_squares(n, bank):
                for k in range(KC):
                    pe.wait_ge(sq_ready, KC * (n - 1) + k + 1)
                    mm = pe.matmul(ps[bank][:, 0:TT], ones, sq[:, k, :], start=(k == 0), stop=(k == KC - 1))
                mm.then_inc(ss_ready, 1)

            def project(w, x, ready, per, loaded, banks):
                pe.wait_ge(loaded, 16)
                for b in range(4):
                    for h in range(2):
                        for k in range(KC):
                            if b == h == 0:
                                pe.wait_ge(ready, k // per + 1)
                            mm = pe.matmul(banks[b][:, h * TT:(h + 1) * TT],
                                           w[:, k, :].rearrange("p (m q) -> p q m", q=KC)[:, 2 * b + h, :],
                                           x[:, k, :], start=(k == 0), stop=(k == KC - 1))
                    mm.then_inc(pj_out, 1)

            pe.wait_ge(ld_const, 16)
            pe.wait_ge(ld_x, 32)
            for b in range(4):
                for h in range(2):
                    for g in range(G):
                        mm = pe.transpose(ps[3 + b][:, (2 * h + g) * T:(2 * h + g + 1) * T],
                                          xtok[:, g, :].rearrange("p (m q) -> p q m", q=KC)[:, 2 * b + h, :], ident)
                mm.then_inc(x_tr, 1)
            pe.wait_ge(ld_rows, 64)
            for cc in range(KC):
                pe.transpose(ps[7][:, cc * TAPS:(cc + 1) * TAPS], dwrow[0:TAPS, cc * P:(cc + 1) * P],
                             ident[0:TAPS, 0:TAPS])
            pe.transpose(ps[7][:, KC * TAPS:KC * TAPS + 4 * KC], crow[0:4 * KC, :], ident[0:4 * KC, 0:4 * KC]
                         ).then_inc(rows_tr, 1)
            pe.wait_ge(rows_in, 1)
            sum_squares(1, 7)
            pe.wait_ge(cond_ready, 1)
            ada_products(range(KC), ps[0])
            ada_transposes(0, ps[0])

            for l in range(L):
                if l == 1:
                    sum_squares(4, 0)
                if l == 0:
                    first_unit = [KC, KC, KC, KC + 2, KC + 6, KC + 10, KC + 14, KC + 19, EARLY]
                    for n, cc in enumerate(CONV_ORDER):
                        if n >= 4:
                            pe.wait_ge(cv_in, n - 3)
                        pe.wait_ge(ld_w1[cc], 32)
                        for h in range(2):
                            for k in range(KC):
                                if n == h == 0:
                                    for g in range(G):
                                        pe.wait_ge(h_ready[g], k + 1)
                                mm = pe.matmul(ps[3 + n % 4][:, h * TT:(h + 1) * TT],
                                               w1[:, k, h * D + cc * P:h * D + (cc + 1) * P],
                                               hT[:, k, :], start=(k == 0), stop=(k == KC - 1))
                        mm.then_inc(cv_u, 1)
                        if n == 4:
                            pe.wait_ge(cv_diag, 1)
                            pe.wait_ge(cv_in, CONV_ORDER.index(PE_CHUNK) + 1)
                            for j in range(TAPS):
                                mm = pe.matmul(ps[7][:, 0:TT].rearrange("p (g t) -> p g t", g=G), diag(j),
                                               upad[:, PE_CHUNK, :, j:j + T], start=(j == 0), stop=(j == TAPS - 1))
                            mm.then_inc(cv_pe, 1)
                        for u in range(first_unit[n], first_unit[n + 1]):
                            if u == 3 * KC:
                                pe.wait_ge(mod_ready, 1)
                            ada_products([u], ps[u // KC % 3])
                    for e in range(1, 4):
                        ada_transposes(e, ps[e % 3])
                    pe.wait_ge(cv_pe_out, 1)
                    sum_squares(2, 7)
                    project(w2, dwo, cn_ready, 1, ld_w2, CB)
                else:
                    pe.wait_ge(ld_qkv, 16)
                    def qkv_product(g, n):
                        for k in range(KC):
                            if n == 0:
                                pe.wait_ge(h_ready[g], 2 * KC + k + 1)
                            mm = pe.matmul(ps[3 * g + n][:, :], hT[:, k, g * T:(g + 1) * T],
                                           wqkv[:, k, n * 512:(n + 1) * 512], start=(k == 0), stop=(k == KC - 1))
                        mm.then_inc(at_qkv, 1)

                    def qk_transposes(g, banks):
                        pe.wait_ge(at_nrm, g + 1)
                        for b, bank in enumerate(banks):
                            for q in range(4 if b < 2 else 2):
                                mm = pe.transpose(bank[:, q * P:(q + 1) * P],
                                                  qkv[:, g, b * 512 + q * P:b * 512 + (q + 1) * P], ident)
                            mm.then_inc(at_tr, 1)

                    for n in range(3):
                        qkv_product(0, n)
                    qkv_product(1, 0)
                    qkv_product(1, 1)
                    pe.wait_ge(ld_kv, 32)
                    for j in range(2):
                        mm = pe.transpose(ps[6][:, j * P:(j + 1) * P], kctx[:, j * P:(j + 1) * P], ident)
                    mm.then_inc(at_tr, 1)
                    qk_transposes(0, ps[0:3])
                    qkv_product(1, 2)
                    def at_scores(i):
                        g, j = divmod(i, NKV)
                        keys = T if g == 0 else 2 * T
                        k0 = 0 if g == 0 else T
                        o = HD * (j % 2)
                        bk = 2 * (i % 2)
                        if i in (0, NKV):
                            pe.wait_ge(at_trc, 4 if i == 0 else 7)
                        if i == 1:
                            pe.wait_ge(at_copied, 2)
                        if i >= 2:
                            pe.wait_ge(at_exp, i - 1)
                        for q in range(QG):
                            mm = pe.matmul(ps[bk + q // 2][:, (q % 2) * 256:(q % 2) * 256 + keys],
                                           qTt[o:o + HD, (j // 2) * QG + q, g * T:(g + 1) * T],
                                           kTt[o:o + HD, j // 2, k0:k0 + keys], start=True, stop=True)
                        mm.then_inc(at_s, 1)

                    def at_transposes(i):
                        nk = 1 if i < NKV else 2
                        pe.wait_ge(at_exp, i + 1)
                        if i == 2:
                            pe.wait_ge(at_trc, 7)
                        for kk in range(nk):
                            for q in range(QG):
                                mm = pe.transpose(ps[4 + kk][:, q * T:(q + 1) * T],
                                                  prob[:, i % 2, q, kk * T:(kk + 1) * T], ident)
                        mm.then_inc(at_pt, 1)

                    def at_values(i):
                        g, j = divmod(i, NKV)
                        nk = 1 if g == 0 else 2
                        pe.wait_ge(at_ptc, i + 1)
                        if i >= 1:
                            pe.wait_ge(at_on, i)
                        for q in range(QG):
                            for kk in range(nk):
                                v = (qkv[:, g, (NH + NKV + j) * HD:(NH + NKV + j + 1) * HD] if kk == 0
                                     else vctx[:, j * HD:(j + 1) * HD])
                                mm = pe.matmul(ps[6][:, q * HD:(q + 1) * HD],
                                               probT[:, kk, q * T:(q + 1) * T], v,
                                               start=(kk == 0), stop=(kk == nk - 1))
                        mm.then_inc(at_o, 1)

                    units = {i: range(36 + i, 37 + i) for i in range(4)}
                    units |= {5: range(40, 43), 6: range(43, 46), 7: range(46, 48)}
                    pe.wait_ge(y_ready, KC)
                    at_scores(0)
                    at_scores(1)
                    ada_products(range(EARLY, EARLY + 4), ps[7])
                    for i in range(G * NKV):
                        at_transposes(i)
                        if i + 2 < G * NKV:
                            at_scores(i + 2)
                        if i == 4:
                            ada_transposes(4, ps[7])
                        if i == 5:
                            pe.wait_ge(mod_ready, 5)
                        ada_products(units.get(i, []), ps[7])
                        at_values(i)
                        if i == 1:
                            pe.wait_ge(at_on, 2)
                            qk_transposes(1, [ps[4], ps[5], ps[6]])
                    pe.wait_ge(at_on, G * NKV)
                    for b in range(4):
                        for h in range(2):
                            for g in range(G):
                                mm = pe.transpose(
                                    ps[b][:, (2 * h + g) * T:(2 * h + g + 1) * T],
                                    otok[:, g, :].rearrange("p (m q) -> p q m", q=KC)[:, 2 * b + h, :], ident)
                        mm.then_inc(at_ot, 1)
                    ada_transposes(5, ps[7])
                    project(wo, oT, at_otc, 2, ld_wo, AB)

                if l == 1:
                    pe.wait_ge(mod_ready, 6)
                sum_squares(3 if l == 0 else 5, 7)
                pe.wait_ge(root_ready, 3 if l == 0 else 5)
                for g in range(G):
                    for k in range(KC):
                        pe.wait_ge(h_ready[g], (2 * l + 1) * KC + k + 1)
                        mm = pe.matmul(ps[7][:, g * NE:(g + 1) * NE], hT[:, k, g * T:(g + 1) * T], rw[:, l, k, :],
                                       start=(k == 0), stop=(k == KC - 1))
                mm.then_inc(rt_logits, 1)
                for g in range(G):
                    for h in range(2):
                        for k in range(4):
                            mm = pe.transpose(ps[2 * g + h][:, k * P:(k + 1) * P],
                                              hT[:, 4 * h + k, g * T:(g + 1) * T], ident)
                        mm.then_inc(ht_tr, 1)
                pe.wait_ge(ld_sh, 48 * (l + 1))
                def shared_hidden(i):
                    w = (gate_of(shw) if i < 2 else up_of(shw)).rearrange("p k (m j) -> p k j m", j=FC)
                    for k in range(KC):
                        mm = pe.matmul(ps[4 + i // 2][:, (i % 2) * TT:(i % 2 + 1) * TT], w[:, k, i % 2, :],
                                       hT[:, k, :], start=(k == 0), stop=(k == KC - 1))
                    return mm

                shared_hidden(0)
                shared_hidden(1)
                pe.wait_ge(rt_sel, l + 1)
                pe.matmul(ps[7][:, 0:NE], ubf[:, 0, :], selb[:, 0, :], start=True, stop=True)
                pe.matmul(ps[7][:, NE:2 * NE], ubf[:, 1, :], selb[:, 0, :], start=True, stop=False)
                pe.matmul(ps[7][:, NE:2 * NE], ubf[:, 0, :], selb[:, 1, :], start=False, stop=True)
                for g in range(G):
                    mm = pe.matmul(ps[7][0:NE, 2 * NE:2 * NE + 2], selb[:, g, :], ubf[:, 1, 0:2],
                                   start=(g == 0), stop=(g == G - 1))
                mm.then_inc(rt_rank, 1)
                shared_hidden(2)
                pe.wait_ge(rt_nov, l + 1)
                pe.matmul(ps[7][:, 0:NE], novb[:, :], ubf[0:NE, 0, 0:NE], start=True, stop=True)
                pe.matmul(ps[7][0:NE, NE:NE + 2], ubf[0:NE, 0, 0:NE], novb[:, 0:2], start=True, stop=True)
                mm = pe.matmul(ps[7][0:1, 2 * NE:2 * NE + 2], ubf[0:NE, 1, 0:1], novb[:, 0:2], start=True, stop=True)
                mm.then_inc(rt_pos, 1)
                shared_hidden(3).then_inc(sh_gu, 1)
                pe.wait_ge(rt_list, l + 1)
                pe.matmul(ps[7][0:1, 0:MAXOVF], ubf[0:NE, 1, 0:1], ovl[:, :],
                          start=True, stop=True).then_inc(rt_tab, 1)

                def shared_down():
                    pe.wait_ge(sh_hid, l + 1)
                    pe.wait_ge(rt_table, l + 1)
                    for k in range(KC):
                        for j in range(FC):
                            mm = pe.matmul(acc[k // 2][:, (k % 2) * TT:(k % 2 + 1) * TT],
                                           down_of(shw)[:, j, :].rearrange("p (m q) -> p q m", q=KC)[:, k, :],
                                           shh[:, 2 + j, :], start=(k % 2 == 0 and j == 0), stop=False,
                                           skip_group_check=True)
                    mm.then_inc(sh_done, 1)

                def gather(i, half):
                    for kk in range(4):
                        for n, (g, part) in enumerate((g, part) for g in range(G) for part in range(3)):
                            mm = pe.matmul(PG[:, kk * P:(kk + 1) * P], hbf[:, part, g, 4 * half + kk, :],
                                           gbf[:, g, :], start=(n == 0), stop=(n == 2 * 3 - 1))
                    mm.then_inc(pe_gather[l], 1)

                def weights_of(half):
                    if half is None:
                        return extra, ld_gu_x[l], ld_dn_x[l]
                    return ([ring[:, 2 * half + b, :] for b in range(2)], ld_gu[l][2 * half:2 * half + 2],
                            ld_dn[l][2 * half:2 * half + 2])

                def gate_up(i, half, fill):
                    w, loaded, _ = weights_of(half)
                    pe.wait_ge(act_xg[l], 2 * i + 2)
                    for b in range(2):
                        pe.wait_ge(loaded[b], 32 * fill)
                    for k in range(KC):
                        for b in range(2):
                            mm = pe.matmul(PGU[64 * b:64 * b + 64, :].rearrange("p (h f) -> p h f", h=2),
                                           xg[:, k, 64 * b:64 * b + 64], gate_up_of(w[b])[:, k],
                                           start=(k == 0), stop=(k == KC - 1))
                    mm.then_inc(pe_gu[l], 1)

                def combine_t(i):
                    for g in range(G):
                        pe.matmul(PT[:, 0:6], gbf[:, g, :], wst[:, g, :, :].rearrange("p s b -> p (s b)"),
                                  start=(g == 0), stop=(g == G - 1))
                    for g in range(G):
                        mm = pe.matmul(PT[:, 256 + g * T:256 + (g + 1) * T], gbf[:, g, :], identb,
                                       start=True, stop=True)
                    mm.then_inc(pe_ct[l], 1)

                def hidden_t(i):
                    pe.wait_ge(dve_h[l], i + 1)
                    pe.wait_ge(dve_c[l], i + 1)
                    for j in range(FC):
                        mm = pe.transpose(PT[:, j * P:(j + 1) * P],
                                          hid.rearrange("p (m j) -> p j m", j=FC)[:, j, :], ident)
                    mm.then_inc(pe_ht[l], 1)

                def down(i, half, fill):
                    w, _, loaded = weights_of(half)
                    pe.wait_ge(dve_ht[l], i + 1)
                    for b in range(2):
                        pe.wait_ge(loaded[b], 16 * fill)
                    for n, bank in ((1, PGU), (0, PY)):
                        for j in range(FC):
                            for b in range(2):
                                mm = pe.matmul(bank[64 * b:64 * b + 64, :], hidT[:, j, 64 * b:64 * b + 64],
                                               down_of(w[b])[:, j, n * 512:(n + 1) * 512],
                                               start=(j == 0), stop=(j == FC - 1))
                        mm.then_inc(pe_dn[l], 1)

                def combine(i, par):
                    pe.wait_ge(dve_y[l], i + 1)
                    pe.wait_ge(act_y2[l], 2 * i + 2)
                    for k in range(KC):
                        for part in range(3):
                            pe.matmul(acc[k // 2][:, (k % 2) * TT:(k % 2 + 1) * TT], y3[:, part, k, :],
                                      comb[:, par, :], start=False, stop=False, skip_group_check=True)

                def pair(i, par, half, fill, first=False, last=False):
                    if not first:
                        pe.wait_ge(dve_rem[l], 2 * i - 1)
                    gate_up(i, half, fill)
                    if not last:
                        pe.wait_ge(dve_g[l], i + 2)
                        gather(i + 1, 0)
                    if not first:
                        combine(i - 1, 1 - par)
                    hidden_t(i)
                    if not last:
                        pe.wait_ge(act_xg[l], 2 * i + 3)
                        gather(i + 1, 1)
                        pe.wait_ge(dve_ht[l], i + 1)
                        combine_t(i + 1)
                    down(i, half, fill)

                pe.wait_ge(ht_done, l + 1)
                pe.wait_ge(dve_g[l], 1)
                gather(0, 0)
                shared_down()
                pe.wait_ge(act_xg[l], 1)
                gather(0, 1)
                combine_t(0)
                pair(0, 0, 0, 1, first=True)
                pair(1, 1, 1, 1)
                pair(2, 0, None, 1)
                nov = pe.value_load(table[0:1, 0:1], min_val=0, max_val=MAXOVF)
                with pe.Fori(0, N_LOOP) as it:
                    for half in range(2):
                        pair(2 * it + half + 3, 1 - half, half, it + 2)
                pair(PAIRS - 1, 1, 0, N_LOOP + 2, last=True)
                combine(PAIRS - 1, 1)
                def overflow_pair(it, par):
                    i = 2 * it + par + PAIRS
                    pe.wait_ge(dve_g[l], i + 1)
                    gather(i, 0)
                    pe.wait_ge(act_xg[l], 2 * i + 1)
                    gather(i, 1)
                    combine_t(i)
                    gate_up(i, 1 - par, it + N_LOOP + 2 + par)
                    hidden_t(i)
                    down(i, 1 - par, it + N_LOOP + 2 + par)
                    combine(i, par)

                with pe.If(nov > 0):
                    overflow_pair(0, 0)
                    with pe.If(nov > 2):
                        overflow_pair(0, 1)
                        with pe.If(nov > 4):
                            with pe.Fori(1, OVF_PAIRS // 2) as it:
                                for par in range(2):
                                    with pe.If(nov > 4 * it + 2 * par):
                                        overflow_pair(it, par)
                pe.matmul(PG[:, 0:2], ones, ones[:, 0:2], start=True, stop=True).then_inc(moe_done, 1)

            pe.wait_ge(y_ready, L * KC)
            for g in range(G):
                for h in range(2):
                    for k in range(4):
                        mm = pe.transpose(ps[2 * g + h][:, k * P:(k + 1) * P],
                                          yT[:, 4 * h + k, g * T:(g + 1) * T], ident)
                    mm.then_inc(y_tr, 1)

        @block.scalar
        def _(act):
            steps = [0]

            def step(ins):
                steps[0] += 1
                ins.then_inc(act_step, 1)
                act.wait_ge(act_step, steps[0])

            act.wait_ge(ld_cond, 32)
            act.wait_ge(cond_zero, 1)
            act.activation(scT[:, :, 0:2], cT[:, :, :].rearrange("p c k -> p k c"), ACT.Silu).then_inc(cond_ready, 1)
            for b in range(4):
                act.wait_ge(x_tr, b + 1)
                act.activation(yT[:, 2 * b:2 * b + 2, :].rearrange("p k t -> p (k t)"), ps[3 + b][:, :],
                               ACT.Copy).then_inc(x_in, 1)

            def ada_copy(e, bank):
                act.wait_ge(ada_used, KC * (e + 1))
                act.activation(arow[:, e % 3, :], bank[:, :], ACT.Copy).then_inc(ada_rows, 1)

            def squares(src, n, ready, value, bank=7):
                for k in range(KC):
                    if ready is cv_out and k == PE_CHUNK:
                        act.wait_ge(cv_pe_out, 1)
                    else:
                        act.wait_ge(ready, value(k))
                    act.activation(sq[:, k, :], src[:, k, :], ACT.Square).then_inc(sq_ready, 1)
                act.wait_ge(ss_ready, n)
                act.activation(rstd[:, :], ps[bank][:, 0:TT], ACT.Sqrt, bias=epsc[:, 0:1], scale=1.0 / D
                               ).then_inc(root_ready, 1)

            def affine(l, which):
                act.wait_ge(mod_ready, 3 * l + (1 if which == 0 else 3))
                for k in range(KC):
                    act.wait_ge(nr_ready, (2 * l + which) * KC + k + 1)
                    v = hT[:, k, 0:T]
                    act.activation(v, v, ACT.Identity, scale=modA[:, l, which, 0, k:k + 1],
                                   bias=mod[:, l, 0, 3 * which * KC + k:3 * which * KC + k + 1]
                                   ).then_inc(h_ready[0], 1)

            for l in range(L):
                if l == 0:
                    squares(yT, 1, x_in, lambda k: k // 2 + 1)
                    ada_copy(0, ps[0])
                else:
                    squares(yT, 4, y_ready, lambda k: k + 1, bank=0)
                affine(l, 0)
                if l == 0:
                    for n, cc in enumerate(CONV_ORDER):
                        act.wait_ge(cv_u, n + 1)
                        if n == 0:
                            act.wait_ge(rows_in, 1)
                        if n >= 2:
                            act.wait_ge(cv_in, n - 1)
                        act.activation(sgt[:, n % 2, :], ps[3 + n % 4][:, TT:2 * TT], ACT.Sigmoid,
                                       bias=cch[:, 1, cc:cc + 1]).then_inc(cv_gate, 1)
                        if n in (1, 2, 3):
                            for j in range(11 * (n - 1), min(11 * n, TAPS)):
                                ins = act.activation(diag(j), ident, ACT.Identity,
                                                     scale=dwc[:, PE_CHUNK, j:j + 1])
                            if n == 3:
                                ins.then_inc(cv_diag, 1)
                    act.wait_ge(cv_pe, 1)
                    act.activation(dwo[:, PE_CHUNK, :], ps[7][:, 0:TT], ACT.Identity,
                                   bias=cch[:, 2, PE_CHUNK:PE_CHUNK + 1]).then_inc(cv_pe_out, 1)
                    act.wait_ge(cv_u, KC)
                    for e in range(1, 4):
                        ada_copy(e, ps[e % 3])
                    squares(dwo, 2, cv_out, lambda k: k + 1)
                    for cc in range(KC):
                        act.wait_ge(cn_scaled, cc + 1)
                        act.activation(dwo[:, cc, :], dwo[:, cc, :], ACT.Silu, scale=cch[:, 3, cc:cc + 1]
                                       ).then_inc(cn_ready, 1)
                    act.wait_ge(ld_small, 16 * N_SMALL)
                    for k in range(KC):
                        act.wait_ge(pj_out, k // 2 + 1)
                        if k >= 2:
                            act.wait_ge(pj_done, k - 1)
                        act.activation(tmp2[:, k % 2, :], CB[k // 2][:, (k % 2) * TT:(k % 2 + 1) * TT],
                                       ACT.Identity, bias=b2c[:, k:k + 1]).then_inc(pj_bias, 1)
                else:
                    def qkv_copies(g):
                        for n in range(3):
                            act.wait_ge(at_qkv, 3 * g + n + 1)
                            dst, src = qkv[:, g, n * 512:(n + 1) * 512], ps[3 * g + n][:, :]
                            if n < 2:
                                dst = dst.rearrange("p (q o d) -> p q o d", o=2, q=QG)
                                src = src.rearrange("p (o q d) -> p q o d", o=2, q=QG)
                            ins = act.activation(dst, src, ACT.Copy)
                        ins.then_inc(at_copied, 1)

                    def qk_roots(g):
                        act.wait_ge(at_qk, g + 1)
                        act.activation(stat[:, 20 * g:20 * g + 20], stat[:, 20 * g:20 * g + 20], ACT.Sqrt,
                                       bias=epsc[:, 0:1], scale=1.0 / HD).then_inc(at_root, 1)

                    def qk_copies(g, banks):
                        for b, bank in enumerate(banks):
                            act.wait_ge(at_tr, 3 * g + b + 2)
                            if b < 2:
                                act.activation(qTt[:, 4 * b:4 * b + 4, g * T:(g + 1) * T],
                                               bank[:, :].rearrange("p (c t) -> p c t", c=4), ACT.Copy
                                               ).then_inc(at_trc, 1)
                            else:
                                act.activation(kTt[:, :, g * T:(g + 1) * T],
                                               bank[:, 0:256].rearrange("p (c t) -> p c t", c=2), ACT.Copy
                                               ).then_inc(at_trc, 1)

                    qkv_copies(0)
                    qk_roots(0)
                    act.wait_ge(at_tr, 1)
                    act.activation(kTt[:, :, 2 * T:3 * T], ps[6][:, 0:256].rearrange("p (c t) -> p c t", c=2),
                                   ACT.Copy).then_inc(at_trc, 1)
                    qk_copies(0, ps[0:3])
                    qkv_copies(1)
                    qk_roots(1)

                    def exps(i):
                        g, j = divmod(i, NKV)
                        keys = T if g == 0 else 2 * T
                        act.wait_ge(at_max, i + 1)
                        if i >= 2:
                            act.wait_ge(at_pt, i - 1)
                        sk = stat[:, 112 + 4 * i:116 + 4 * i]
                        act.activation(sk, sk, ACT.Exp)
                        for q in range(QG):
                            m = 40 + 4 * i + q
                            ins = act.activation(prob[:, i % 2, q, 0:keys],
                                                 ps[2 * (i % 2) + q // 2][:, (q % 2) * 256:(q % 2) * 256 + keys],
                                                 ACT.Exp, bias=stat[:, m:m + 1], scale=HD ** -0.5,
                                                 accum_out=stat[:, 32 + m:32 + m + 1])
                        ins.then_inc(at_exp, 1)

                    for i in range(G * NKV):
                        exps(i)
                        if i == 2:
                            qk_copies(1, [ps[4], ps[5], ps[6]])
                        if i == 4:
                            ada_copy(4, ps[7])
                    ada_copy(5, ps[7])
                    for b in range(4):
                        act.wait_ge(at_ot, b + 1)
                        act.activation(oT[:, 2 * b:2 * b + 2, :].rearrange("p k t -> p (k t)"), ps[b][:, :],
                                       ACT.Copy).then_inc(at_otc, 1)
                squares(yT, 3 if l == 0 else 5, pj_done, lambda k: KC * l + k + 1)
                affine(l, 1)
                act.wait_ge(rt_logits, l + 1)
                act.activation(scores[:, :, :].rearrange("p g e -> p (g e)"), ps[7][:, 0:2 * NE], ACT.Sigmoid
                               ).then_inc(rt_score, 1)
                for i in range(4):
                    g, h = divmod(i, 2)
                    act.wait_ge(ht_tr, 4 * l + i + 1)
                    dst = hbf[:, 0, g, 4 * h:4 * h + 4, :].rearrange("p k m -> p (k m)")
                    act.activation(dst, ps[i][:, :], ACT.Copy).then_inc(ht_b1, 1)
                for i in range(4):
                    g, h = divmod(i, 2)
                    act.wait_ge(ht_r1, 4 * l + i + 1)
                    dst = hbf[:, 1, g, 4 * h:4 * h + 4, :].rearrange("p k m -> p (k m)")
                    act.activation(dst, ps[i][:, :], ACT.Copy).then_inc(ht_b2, 1)
                act.wait_ge(sh_gu, l + 1)
                act.activation(shh[:, 0:2, :].rearrange("p j t -> p (j t)"), ps[4][:, :], ACT.Silu).then_inc(sh_silu, 1)

                def gathered(i, half):
                    act.wait_ge(pe_gather[l], 2 * i + half + 1)
                    act.activation(xg[:, 4 * half:4 * half + 4, :].rearrange("p k s -> p (k s)"), PG[:, :], ACT.Copy
                                   ).then_inc(act_xg[l], 1)

                def silu(i):
                    act.wait_ge(pe_gu[l], i + 1)
                    act.activation(silu_h, PGU[:, 0:DE], ACT.Silu).then_inc(act_silu[l], 1)

                def y_parts(i):
                    for h, src in enumerate((PGU[:, :], PY[:, :])):
                        act.wait_ge(pe_dn[l], 2 * i + 1 + h)
                        act.activation(half_of(y3[:, 0], h), src.rearrange("p (m k) -> p m k", k=KC), ACT.Copy
                                       ).then_inc(act_y1[l], 1)
                    for h, src in enumerate((yrem, PY[:, :])):
                        act.wait_ge(dve_rem[l], 2 * i + 1 + h)
                        act.activation(half_of(y3[:, 1], h), src.rearrange("p (m k) -> p m k", k=KC), ACT.Copy
                                       ).then_inc(act_y2[l], 1)

                def pair(i, last=False):
                    silu(i)
                    if not last:
                        gathered(i + 1, 0)
                        gathered(i + 1, 1)
                    y_parts(i)

                gathered(0, 0)
                gathered(0, 1)
                for i in range(3):
                    pair(i)
                act.wait_ge(rt_table, l + 1)
                nov = act.value_load(table[0:1, 0:1], min_val=0, max_val=MAXOVF)
                with act.Fori(0, N_LOOP) as it:
                    for half in range(2):
                        pair(2 * it + half + 3)
                pair(PAIRS - 1, last=True)
                def overflow_pair(it, par):
                    i = 2 * it + par + PAIRS
                    gathered(i, 0)
                    gathered(i, 1)
                    silu(i)
                    y_parts(i)

                with act.If(nov > 0):
                    overflow_pair(0, 0)
                    with act.If(nov > 2):
                        overflow_pair(0, 1)
                        with act.If(nov > 4):
                            with act.Fori(1, OVF_PAIRS // 2) as it:
                                for par in range(2):
                                    with act.If(nov > 4 * it + 2 * par):
                                        overflow_pair(it, par)

            for g in range(G):
                for h in range(2):
                    act.wait_ge(y_tr, 2 * g + h + 1)
                    dst = ytok[:, g, :].rearrange("p (m k) -> p k m", k=KC)[:, 4 * h:4 * h + 4, :]
                    act.activation(dst, ps[2 * g + h][:, :].rearrange("p (k m) -> p k m", k=4), ACT.Copy
                                   ).then_inc(y_out, 1)

        @block.vector
        def _(dve):
            steps = [0]

            def step(ins):
                steps[0] += 1
                ins.then_inc(dve_step, 1)
                dve.wait_ge(dve_step, steps[0])

            dve.memset(epsc[:, :], EPS)
            dve.memset(scT[:, :, 2:32], 0.0).then_inc(cond_zero, 1)
            dve.wait_ge(ld_const, 16)
            dve.tensor_copy(ubf[:, 0, :], cst[:, C_U:C_U + P])
            dve.tensor_copy(ubf[:, 1, :], ones)
            dve.wait_ge(rows_tr, 1)
            dve.tensor_copy(dwc[:, :, :].rearrange("p c j -> p (c j)"), ps[7][:, 0:KC * TAPS])
            dve.tensor_copy(cch[:, :, :].rearrange("p i c -> p (i c)"), ps[7][:, KC * TAPS:KC * TAPS + 4 * KC]
                            ).then_inc(rows_in, 1)
            dve.wait_ge(ld_mod0, 48)

            def ada_finish(e, bank):
                l, b = divmod(e, 3)
                dve.wait_ge(ada_cols, e + 1)
                for cd in range(2):
                    src = bank[:, :].rearrange("p (q j r) -> p j q r", q=4, j=4)[:, :, :, cd]
                    ins = dve.tensor_tensor(
                        mod[:, l, cd, 16 * b:16 * b + 16].rearrange("p (j q) -> p j q", j=4), src,
                        adab[:, l, 2 * b:2 * b + 2, :].rearrange("p s (j q) -> p (s j) q", j=2), ALU.add)
                if b != 1:
                    step(ins)
                    which = b // 2
                    s = 1 + 3 * which
                    for cd in range(2):
                        ins = dve.scalar_tensor_tensor(modA[:, l, which, cd, :], mod[:, l, cd, s * KC:(s + 1) * KC],
                                                       1.0, gains[:, l, which, :], ALU.add, ALU.mult)
                ins.then_inc(mod_ready, 1)

            def normalise(l, which):
                dve.wait_ge(mod_ready, 3 * l + (1 if which == 0 else 3))
                dve.wait_ge(root_ready, norms[0] + 1)
                norms[0] += 1
                step(dve.reciprocal(rstd[:, :], rstd[:, :]))
                first = (2 * l + which) * KC
                for k in range(KC + 1):
                    if k < KC:
                        dve.tensor_tensor(hT[:, k, :], yT[:, k, :], rstd[:, :], ALU.mult).then_inc(nr_ready, 1)
                    if k >= 1:
                        dve.wait_ge(nr_ready, first + k)
                        v = hT[:, k - 1, T:2 * T]
                        dve.tensor_scalar(v, v, modA[:, l, which, 1, k - 1:k],
                                          mod[:, l, 1, 3 * which * KC + k - 1:3 * which * KC + k],
                                          ALU.mult, ALU.add).then_inc(h_ready[1], 1)

            norms = [0]
            dve.wait_ge(x_in, 4)
            ada_finish(0, ps[0])
            for l in range(L):
                normalise(l, 0)
                if l == 0:
                    dve.wait_ge(rows_in, 1)
                    dve.memset(upad[:, :, :, 0:PAD], 0.0)
                    step(dve.memset(upad[:, :, :, PAD + T:], 0.0))
                    def gated(n):
                        cc = CONV_ORDER[n]
                        dve.wait_ge(cv_gate, n + 1)
                        dve.scalar_tensor_tensor(
                            upad[:, cc, :, PAD:PAD + T], ps[3 + n % 4][:, 0:TT].rearrange("p (g t) -> p g t", g=G),
                            cch[:, 0, cc:cc + 1], sgt[:, n % 2, :].rearrange("p (g t) -> p g t", g=G),
                            ALU.add, ALU.mult).then_inc(cv_in, 1)

                    def convolve(cc):
                        outs = [dwo[:, cc, :].rearrange("p (g t) -> p g t", g=G),
                                odd.rearrange("p (g t) -> p g t", g=G)]
                        for j in range(TAPS):
                            o, x, tap = outs[j % 2], upad[:, cc, :, j:j + T], dwc[:, cc, j:j + 1]
                            if j == 0:
                                ins = dve.tensor_scalar(o, x, tap, cch[:, 2, cc:cc + 1], ALU.mult, ALU.add)
                            elif j == 1:
                                ins = dve.tensor_scalar(o, x, tap, None, ALU.mult)
                            else:
                                dve.wait_ge(dve_step, steps[0] - 1)
                                ins = dve.scalar_tensor_tensor(o, x, tap, o, ALU.mult, ALU.add)
                            steps[0] += 1
                            ins.then_inc(dve_step, 1)
                        dve.wait_ge(dve_step, steps[0])
                        dve.tensor_tensor(outs[0], outs[0], outs[1], ALU.add).then_inc(cv_out, 1)

                    for n, cc in enumerate(CONV_ORDER):
                        if cc == PE_CHUNK:
                            continue
                        gated(n)
                        dve.wait_ge(cv_in, n + 1)
                        convolve(cc)
                        if CONV_ORDER[(n + 1) % KC] == PE_CHUNK:
                            gated(n + 1)
                    dve.wait_ge(ld_small, 16 * N_SMALL)
                    for e in range(1, 4):
                        ada_finish(e, ps[e % 3])
                    dve.wait_ge(mod_ready, 4)
                    dve.wait_ge(root_ready, 2)
                    norms[0] += 1
                    step(dve.reciprocal(rstd[:, :], rstd[:, :]))
                    for cc in range(KC):
                        dve.tensor_tensor(dwo[:, cc, :], dwo[:, cc, :], rstd[:, :], ALU.mult).then_inc(cn_scaled, 1)
                    for k in range(KC):
                        dve.wait_ge(pj_bias, k + 1)
                        for g in range(G):
                            v = yT[:, k, g * T:(g + 1) * T]
                            ins = dve.scalar_tensor_tensor(v, tmp2[:, k % 2, g * T:(g + 1) * T],
                                                           mod[:, l, g, 2 * KC + k:2 * KC + k + 1], v,
                                                           ALU.mult, ALU.add)
                        ins.then_inc(pj_done, 1)
                else:
                    nqk = NH + NKV
                    for g in range(G):
                        dve.wait_ge(at_copied, g + 1)
                        v = qkv[:, g, 0:nqk * HD]
                        v3 = v.rearrange("p (h d) -> p h d", d=HD)
                        st = stat[:, nqk * g:nqk * (g + 1)]
                        step(dve.tensor_tensor(asq[:, g, :], v, v, ALU.mult))
                        dve.tensor_reduce(st, asq[:, g, :].rearrange("p (h d) -> p h d", d=HD), AX_X, ALU.add
                                          ).then_inc(at_qk, 1)
                        dve.wait_ge(at_root, g + 1)
                        step(dve.reciprocal(st, st))
                        step(dve.tensor_tensor(v3, v3, st[:, :, None].to_broadcast([P, nqk, HD]), ALU.mult))
                        dve.tensor_tensor(v3[:, 0:NH, :], v3[:, 0:NH, :],
                                          qkn[:, 0:1, :].to_broadcast([P, NH, HD]), ALU.mult)
                        ins = dve.tensor_tensor(v3[:, NH:, :], v3[:, NH:, :],
                                                qkn[:, 1:2, :].to_broadcast([P, NKV, HD]), ALU.mult)
                        if g == 1:
                            step(ins)
                            r = v.rearrange("p (h r s d) -> p h r s d", r=2, s=2, d=HD // 4)
                            a2 = asq[:, 0, :].rearrange("p (h r s d) -> p h r s d", r=2, s=2, d=HD // 4)
                            b2 = asq[:, 1, :].rearrange("p (h r s d) -> p h r s d", r=2, s=2, d=HD // 4)
                            for ax in range(2):
                                cs = cosT[:, None, 16 * ax:16 * ax + 16].to_broadcast([P, nqk, 16])
                                sn = sinT[:, None, 16 * ax:16 * ax + 16].to_broadcast([P, nqk, 16])
                                for s in range(2):
                                    dve.tensor_tensor(a2[:, :, ax, s], r[:, :, ax, s], cs, ALU.mult)
                                    ins = dve.tensor_tensor(b2[:, :, ax, s], r[:, :, ax, 1 - s], sn, ALU.mult)
                            step(ins)
                            for ax in range(2):
                                dve.tensor_tensor(r[:, :, ax, 0], a2[:, :, ax, 0], b2[:, :, ax, 0], ALU.subtract)
                                ins = dve.tensor_tensor(r[:, :, ax, 1], a2[:, :, ax, 1], b2[:, :, ax, 1], ALU.add)
                        ins.then_inc(at_nrm, 1)

                    def maxima(i):
                        g, j = divmod(i, NKV)
                        keys = T if g == 0 else 2 * T
                        dve.wait_ge(at_s, i + 1)
                        mx = stat[:, 104 + 4 * (i % 2):108 + 4 * (i % 2)]
                        for b in range(2):
                            ins = dve.tensor_reduce(
                                mx[:, 2 * b:2 * b + 2],
                                ps[2 * (i % 2) + b][:, :].rearrange("p (h s) -> p h s", h=2)[:, :, 0:keys],
                                AX_X, ALU.max)
                        step(ins)
                        step(dve.scalar_tensor_tensor(mx, mx, HD ** -0.5, sinkb[:, 4 * j:4 * j + 4],
                                                      ALU.mult, ALU.max))
                        dve.tensor_tensor(stat[:, 112 + 4 * i:116 + 4 * i], sinkb[:, 4 * j:4 * j + 4], mx, ALU.subtract)
                        dve.tensor_scalar(stat[:, 40 + 4 * i:44 + 4 * i], mx, -1.0, None, ALU.mult
                                          ).then_inc(at_max, 1)

                    def prob_copies(i):
                        dve.wait_ge(at_pt, i + 1)
                        for kk in range(1 if i < NKV else 2):
                            ins = dve.tensor_copy(probT[:, kk, :], ps[4 + kk][:, :])
                        ins.then_inc(at_ptc, 1)

                    def outputs(i):
                        g, j = divmod(i, NKV)
                        step(dve.tensor_tensor(stat[:, 72 + 4 * i:76 + 4 * i], stat[:, 72 + 4 * i:76 + 4 * i],
                                               stat[:, 112 + 4 * i:116 + 4 * i], ALU.add))
                        step(dve.reciprocal(stat[:, 72 + 4 * i:76 + 4 * i], stat[:, 72 + 4 * i:76 + 4 * i]))
                        dve.wait_ge(at_o, i + 1)
                        dve.tensor_tensor(
                            otok[:, g, 4 * j * HD:4 * (j + 1) * HD].rearrange("p (h d) -> p h d", h=QG),
                            ps[6][:, 0:QG * HD].rearrange("p (h d) -> p h d", h=QG),
                            stat[:, 72 + 4 * i:76 + 4 * i, None].to_broadcast([P, QG, HD]), ALU.mult
                        ).then_inc(at_on, 1)

                    maxima(0)
                    maxima(1)
                    for i in range(G * NKV):
                        prob_copies(i)
                        outputs(i)
                        if i + 2 < G * NKV:
                            maxima(i + 2)
                        if i == 4:
                            ada_finish(4, ps[7])
                    ada_finish(5, ps[7])
                    dve.wait_ge(mod_ready, 6)
                    for k in range(KC):
                        dve.wait_ge(pj_out, 4 + k // 2 + 1)
                        for g in range(G):
                            v = yT[:, k, g * T:(g + 1) * T]
                            ins = dve.scalar_tensor_tensor(
                                v, AB[k // 2][:, (k % 2) * TT + g * T:(k % 2) * TT + (g + 1) * T],
                                mod[:, l, g, 2 * KC + k:2 * KC + k + 1], v, ALU.mult, ALU.add)
                        ins.then_inc(pj_done, 1)

                normalise(l, 1)
                dve.wait_ge(rt_score, l + 1)
                step(dve.tensor_tensor(choice[:, :, :], scores[:, :, :],
                                       rbias[:, l:l + 1, :].to_broadcast([P, G, NE]), ALU.add))
                for g in range(G):
                    for r in range(NGRP):
                        ins = dve.max(top8[:, g, r, :], choice[:, g, r * EPG:(r + 1) * EPG])
                step(ins)
                step(dve.tensor_tensor(gsc[:, :, :], top8[:, :, :, 0], top8[:, :, :, 1], ALU.add))
                for g in range(G):
                    mine = gsc[:, g, :, None].to_broadcast([P, NGRP, NGRP])
                    other = gsc[:, g, None, :].to_broadcast([P, NGRP, NGRP])
                    dve.tensor_tensor(gcmp[:, g], other, mine, ALU.is_gt)
                    ins = dve.tensor_tensor(gcmp2[:, g], other, mine, ALU.is_equal)
                step(ins)
                for g in range(G):
                    ins = dve.tensor_tensor(gcmp2[:, g], gcmp2[:, g], tri.rearrange("p (a b) -> p a b", a=NGRP), ALU.mult)
                step(ins)
                step(dve.tensor_tensor(gcmp[:, :, :, :], gcmp[:, :, :, :], gcmp2[:, :, :, :], ALU.add))
                step(dve.tensor_reduce(gsc[:, :, :], gcmp[:, :, :, :], AX_X, ALU.add))
                step(dve.tensor_scalar(gsc[:, :, :], gsc[:, :, :], TOPG - 0.5, None, ALU.is_lt))
                gm = [gsc[:, g, :, None].to_broadcast([P, NGRP, EPG]) for g in range(G)]
                for g in range(G):
                    ch = choice[:, g, :].rearrange("p (a b) -> p a b", a=NGRP)
                    dve.tensor_tensor(ch, ch, gm[g], ALU.mult)
                    ins = dve.tensor_scalar(sel[:, g, :].rearrange("p (a b) -> p a b", a=NGRP), gm[g], 1.0, BIG,
                                            ALU.subtract, ALU.mult)
                step(ins)
                step(dve.tensor_tensor(choice[:, :, :], choice[:, :, :], sel[:, :, :], ALU.add))
                for g in range(G):
                    ins = dve.max(top8[:, g, 0, :], choice[:, g, :])
                step(ins)
                for g in range(G):
                    ins = dve.match_replace(sel[:, g, :], top8[:, g, 0, :], choice[:, g, :], -2 * BIG)
                step(ins)
                step(dve.tensor_tensor(sel[:, :, :], sel[:, :, :], choice[:, :, :], ALU.not_equal))
                dve.tensor_copy(selb[:, :, :], sel[:, :, :]).then_inc(rt_sel, 1)
                step(dve.tensor_tensor(wt[:, :, :], scores[:, :, :], sel[:, :, :], ALU.mult))
                step(dve.tensor_reduce(wsum[:, :, 0], wt[:, :, :], AX_X, ALU.add))
                step(dve.reciprocal(wsum[:, :, 1], wsum[:, :, 0]))
                for g in range(G):
                    ins = dve.tensor_scalar(wt[:, g, :], wt[:, g, :], wsum[:, g, 1:2], ROUTED_SCALE,
                                            ALU.mult, ALU.mult)
                step(ins)
                dve.tensor_copy(identb, ident)
                step(dve.tensor_copy(wt3[:, :, 0, :], wt[:, :, :]))
                step(dve.tensor_tensor(choice[:, :, :], wt[:, :, :], wt3[:, :, 0, :], ALU.subtract))
                step(dve.tensor_copy(wt3[:, :, 1, :], choice[:, :, :]))
                step(dve.tensor_tensor(wt3[:, :, 2, :], choice[:, :, :], wt3[:, :, 1, :], ALU.subtract))
                for i in range(4):
                    g, h = divmod(i, 2)
                    dve.wait_ge(ht_b1, 4 * l + i + 1)
                    dve.tensor_tensor(ps[i][:, :], ps[i][:, :],
                                      hbf[:, 0, g, 4 * h:4 * h + 4, :].rearrange("p k m -> p (k m)"), ALU.subtract
                                      ).then_inc(ht_r1, 1)
                dve.wait_ge(rt_rank, l + 1)
                step(dve.scalar_tensor_tensor(rank[:, :, :].rearrange("p g e -> p (g e)"), ps[7][:, 0:2 * NE], 1.0,
                                              sel[:, :, :].rearrange("p g e -> p (g e)"), ALU.add, ALU.mult))
                dve.tensor_scalar(rank[:, :, :], rank[:, :, :], -1.0, None, ALU.add)
                step(dve.tensor_copy(novc[:, 0:1], ps[7][0:NE, 2 * NE:2 * NE + 1]))
                for n in range(3):
                    ins = dve.tensor_scalar(novc[:, 1 + n:2 + n], novc[:, 0:1], (n + 1) * SLOTS + 0.5, None, ALU.is_gt)
                step(ins)
                step(dve.tensor_tensor(novc[:, 4:5], novc[:, 1:2], novc[:, 2:3], ALU.add))
                step(dve.tensor_tensor(novc[:, 4:5], novc[:, 4:5], novc[:, 3:4], ALU.add))
                dve.tensor_scalar(novb[:, :], ones[0:NE, :], novc[:, 4:5], None, ALU.mult).then_inc(rt_nov, 1)
                for i in range(4):
                    g, h = divmod(i, 2)
                    dve.wait_ge(ht_b2, 4 * l + i + 1)
                    ins = dve.tensor_tensor(hbf[:, 2, g, 4 * h:4 * h + 4, :].rearrange("p k m -> p (k m)"), ps[i][:, :],
                                            hbf[:, 1, g, 4 * h:4 * h + 4, :].rearrange("p k m -> p (k m)"),
                                            ALU.subtract)
                ins.then_inc(ht_done, 1)
                dve.wait_ge(rt_pos, l + 1)
                step(dve.tensor_scalar(ovrank[:, 0, :], ps[7][:, 0:NE], 1.0, float(SLOTS), ALU.subtract, ALU.mult))
                step(dve.tensor_copy(ovrank[:, 1, :], ovrank[:, 0, :]))
                dve.tensor_tensor(ovrank[:, :, :], ovrank[:, :, :], rank[:, :, :], ALU.add).then_inc(dve_ov[l], 1)
                step(dve.tensor_tensor(endc[:, :], novc[:, 4:5], ps[7][0:NE, NE:NE + 1], ALU.add))
                dve.tensor_copy(table[0:1, 0:1], ps[7][0:1, 2 * NE:2 * NE + 1])
                dve.tensor_scalar(ovl[:, :], iota[0:NE, 0:MAXOVF], endc[:, 0:1], None, ALU.is_ge).then_inc(rt_list, 1)
                dve.wait_ge(rt_tab, l + 1)
                dve.tensor_scalar(table[0:1, 1:1 + MAXOVF], ps[7][0:1, 0:MAXOVF], NE - 1.0, None, ALU.min
                                  ).then_inc(rt_table, 1)

                def one_hot(i):
                    if type(i) is int:
                        dve.tensor_copy(wst[:, :, :, :], wt3[:, :, :, 2 * i:2 * i + 2])
                    else:
                        dve.tensor_copy(wst[:, :, :, :], wt3[:, :, :, bass.ds(2 * i, 2)])
                    for g in range(G):
                        for b in range(2):
                            r = (rank[:, g, 2 * i + b:2 * i + b + 1] if type(i) is int
                                 else rank[:, g, bass.ds(2 * i + b, 1)])
                            ins = dve.tensor_scalar(gbf[:, g, 64 * b:64 * b + 64], iota, r, None, ALU.is_equal)
                    ins.then_inc(dve_g[l], 1)

                def combine_copy(i, par):
                    dve.wait_ge(pe_ct[l], i + 1)
                    dve.tensor_copy(comb[:, par, :], PT[:, 256:512])
                    for b in range(2):
                        ins = dve.tensor_reduce(
                            wslot[64 * b:64 * b + 64, par:par + 1],
                            PT[64 * b:64 * b + 64, 0:6].rearrange("p (s b) -> p b s", b=2)[:, b, :], AX_X, ALU.add)
                    ins.then_inc(dve_c[l], 1)

                def hidden(i, par):
                    dve.wait_ge(act_silu[l], i + 1)
                    dve.wait_ge(dve_c[l], i + 1)
                    dve.scalar_tensor_tensor(hid, silu_h, wslot[:, par:par + 1], PGU[:, DE:2 * DE],
                                             ALU.mult, ALU.mult).then_inc(dve_h[l], 1)

                def hidden_copy(i):
                    dve.wait_ge(pe_ht[l], i + 1)
                    dve.tensor_copy(hidT.rearrange("p j s -> p (j s)"), PT[:, 0:256]).then_inc(dve_ht[l], 1)

                def y_rest(i):
                    for h, (src, rem) in enumerate(((PGU, yrem), (PY, PY[:, :]))):
                        dve.wait_ge(act_y1[l], 2 * i + 1 + h)
                        dve.tensor_tensor(rem.rearrange("p (m k) -> p m k", k=KC),
                                          src[:, :].rearrange("p (m k) -> p m k", k=KC),
                                          half_of(y3[:, 0], h), ALU.subtract).then_inc(dve_rem[l], 1)
                    for h, rem in enumerate((yrem, PY[:, :])):
                        dve.wait_ge(act_y2[l], 2 * i + 1 + h)
                        ins = dve.tensor_tensor(half_of(y3[:, 2], h), rem.rearrange("p (m k) -> p m k", k=KC),
                                                half_of(y3[:, 1], h), ALU.subtract)
                    ins.then_inc(dve_y[l], 1)

                def pair(i, par, last=False):
                    if not last:
                        one_hot(i + 1)
                    hidden(i, par)
                    hidden_copy(i)
                    if not last:
                        combine_copy(i + 1, 1 - par)
                    y_rest(i)

                one_hot(0)
                dve.wait_ge(sh_silu, l + 1)
                dve.tensor_tensor(shh[:, 2:4, :].rearrange("p j t -> p (j t)"),
                                  shh[:, 0:2, :].rearrange("p j t -> p (j t)"), ps[5][:, :], ALU.mult
                                  ).then_inc(sh_hid, 1)
                combine_copy(0, 0)
                for i in range(3):
                    pair(i, i % 2)
                dve.wait_ge(rt_table, l + 1)
                nov = dve.value_load(table[0:1, 0:1], min_val=0, max_val=MAXOVF)
                with dve.Fori(0, N_LOOP) as it:
                    for half in range(2):
                        pair(2 * it + half + 3, 1 - half)
                pair(PAIRS - 1, 1, last=True)
                def overflow_pair(it, par):
                    i = 2 * it + par + PAIRS
                    j = 2 * it + par
                    e = [dve.value_load(table[0:1, bass.ds(2 * j + b + 1, 1)], min_val=0, max_val=NE - 1)
                         for b in range(2)]
                    dve.wait_ge(dve_ov[l], 3 * j + 1)

                    for b in range(2):
                        dve.tensor_copy(wst[:, :, :, b:b + 1], wt3[:, :, :, bass.ds(e[b], 1)])
                        for g in range(G):
                            ins = dve.tensor_scalar(gbf[:, g, 64 * b:64 * b + 64], iota,
                                                    ovrank[:, g, bass.ds(e[b], 1)], None, ALU.is_equal)
                        if b == 0:
                            ins.then_inc(dve_ov[l], 1)
                            dve.wait_ge(dve_ov[l], 3 * j + 2)
                        else:
                            ins.then_inc(dve_g[l], 1)
                            dve.wait_ge(dve_g[l], i + 1)
                        dve.tensor_scalar(ovrank[:, :, :], ovrank[:, :, :], -float(SLOTS), None, ALU.add
                                          ).then_inc(dve_ov[l], 1)
                        dve.wait_ge(dve_ov[l], 3 * j + b + 3)
                    combine_copy(i, par)
                    hidden(i, par)
                    hidden_copy(i)
                    y_rest(i)

                with dve.If(nov > 0):
                    overflow_pair(0, 0)
                    with dve.If(nov > 2):
                        overflow_pair(0, 1)
                        with dve.If(nov > 4):
                            with dve.Fori(1, OVF_PAIRS // 2) as it:
                                for par in range(2):
                                    with dve.If(nov > 4 * it + 2 * par):
                                        overflow_pair(it, par)
                dve.wait_ge(moe_done, l + 1)
                for k in range(KC):
                    for g in range(G):
                        v = yT[:, k, g * T:(g + 1) * T]
                        ins = dve.scalar_tensor_tensor(
                            v, acc[k // 2][:, (k % 2) * TT + g * T:(k % 2) * TT + (g + 1) * T],
                            mod[:, l, g, 5 * KC + k:5 * KC + k + 1], v, ALU.mult, ALU.add)
                    ins.then_inc(y_ready, 1)


def shape_constants():
    import numpy as np

    a = np.zeros((P, C_W), np.float32)
    a[:, C_ID:C_ID + P] = np.eye(P)
    a[:, C_ONE:C_ONE + P] = 1.0
    a[:, C_U:C_U + P] = np.triu(np.ones((P, P)), 1)
    a[:, C_IOTA:C_IOTA + 64] = np.arange(64)[None, :]
    a[:, C_TRI:C_TRI + 64] = np.tril(np.ones((8, 8)), -1).reshape(1, 64)
    inv = np.float32(10000.0) ** (-np.arange(16, dtype=np.float32) / np.float32(16))
    pos = np.arange(P)
    for ax, at in enumerate((pos // 64, pos % 64)):
        ang = at.astype(np.float32)[:, None] * inv[None, :].astype(np.float32)
        a[:, C_COS + 16 * ax:C_COS + 16 * ax + 16] = np.cos(ang)
        a[:, C_SIN + 16 * ax:C_SIN + 16 * ax + 16] = np.sin(ang)
    return a


_INS = ['x_prompt', 'x_sample', 'cache_k', 'cache_v', 'c', 'c_ctx', 'ada_w', 'ada_b', 'norm_mix', 'norm_ffn',
        'conv_w1', 'conv_b1', 'conv_dw', 'conv_dw_b', 'conv_norm', 'conv_w2', 'conv_b2',
        'attn_wqkv', 'attn_q_norm', 'attn_k_norm', 'attn_sink', 'attn_wo',
        'router_w', 'router_bias', 'exp_w_gate', 'exp_w_up', 'exp_w_down', 'sh_w_gate', 'sh_w_up', 'sh_w_down']
_OUTS = [(1, T, D), (1, T, D), (1, 1, T, NKV, HD), (1, 1, T, NKV, HD)]


def kernel(**inputs):
    import numpy as _np
    import concourse.bacc as _bacc
    from concourse import mybir as _mybir
    from concourse.bass_utils import run_bass_kernel_spmd as _run

    nc = _bacc.Bacc("TRN2", target_bir_lowering=False, num_devices=1)
    arrays, args = {}, []
    for name in _INS:
        a = _np.ascontiguousarray(inputs[name])
        arrays[f"in_{name}_dram"] = a
        args.append(nc.dram_tensor(f"in_{name}_dram", a.shape, _mybir.dt.from_np(a.dtype), kind="ExternalInput").ap())
    a = shape_constants()
    arrays["in_consts_dram"] = a
    args.append(nc.dram_tensor("in_consts_dram", a.shape, F32, kind="ExternalInput").ap())
    for i, shape in enumerate(_OUTS):
        args.append(nc.dram_tensor(f"out_{i}_dram", shape, F32, kind="ExternalOutput").ap())
    build_kernel(nc, *args)
    r = _run(nc, [arrays], core_ids=[0])
    return tuple(r.results[0][f"out_{i}_dram"] for i in range(len(_OUTS)))
```
